# Optimizing a Trainium2 kernel written in Bass

```python
import math
import jax, jax.numpy as jnp
from jax import lax
import numpy as np

D_MODEL = 1024
BATCH = 1
SEQ = 4096
DEPTH = 1
DEC_BATCH = 8
DEC_SEQ = 16
PAST_LEN = 1024

CHUNK = 64
CONV_W = 4
LRU_WIDTH = 512
LRU_BLOCKS = 8
LRU_BLOCK = LRU_WIDTH // LRU_BLOCKS
LRU_C = 8.0
GDN_HEADS = 4
GDN_DK = 128
GDN_DV = 128
GDN_QK = GDN_HEADS * GDN_DK
GDN_V = GDN_HEADS * GDN_DV
GDN_CONV_CH = 2 * GDN_QK + GDN_V
MIX_WIDTH = LRU_WIDTH + GDN_V
IN_COLS = 2 * LRU_WIDTH + GDN_CONV_CH + GDN_V + 2 * GDN_HEADS
N_GROUPS = 4
EXPERTS_PER_GROUP = 8
N_EXPERTS = N_GROUPS * EXPERTS_PER_GROUP
TOP_K = 2
D_EXPERT = 256
ROW_BLOCK = 128
EPS = 1e-6

kernel_name = 'hybrid_rglru_gdn_hmoe_stream_step'

def rmsnorm(x, g):
    xf = x.astype(jnp.float32)
    y = xf * lax.rsqrt(jnp.mean(xf * xf, axis=-1, keepdims=True) + EPS)
    return (y * g.astype(jnp.float32)).astype(x.dtype)

def l2norm(x):
    return x * lax.rsqrt(jnp.sum(x * x, axis=-1, keepdims=True) + EPS)

def causal_conv(x, prev, w):
    L = x.shape[1]
    xp = jnp.concatenate([prev.astype(x.dtype), x], axis=1)
    out = xp[:, 0:L] * w[0]
    for j in range(1, CONV_W):
        out = out + xp[:, j:j + L] * w[j]
    return out, xp[:, xp.shape[1] - (CONV_W - 1):]

def rglru(xc, h0, wa, ba, wx, bx, lam):
    B, L, _ = xc.shape
    xf = xc.astype(jnp.float32)
    xb = xf.reshape(B, L, LRU_BLOCKS, LRU_BLOCK)
    r = jax.nn.sigmoid(jnp.einsum('blni,nij->blnj', xb, wa.astype(jnp.float32)).reshape(B, L, LRU_WIDTH) + ba.astype(jnp.float32))
    i = jax.nn.sigmoid(jnp.einsum('blni,nij->blnj', xb, wx.astype(jnp.float32)).reshape(B, L, LRU_WIDTH) + bx.astype(jnp.float32))
    log_a = -LRU_C * r * jax.nn.softplus(-lam.astype(jnp.float32))
    a = jnp.exp(log_a)
    b = jnp.sqrt(-jnp.expm1(2.0 * log_a)) * (i * xf)

    def combine(c1, c2):
        a1, b1 = c1
        a2, b2 = c2
        return a1 * a2, a2 * b1 + b2

    a_cum, b_cum = lax.associative_scan(combine, (a, b), axis=1)
    h = a_cum * h0.astype(jnp.float32)[:, None, :] + b_cum
    return h, h[:, -1]

def gdn_chunk(S, q, k, v, g, beta):
    L = q.shape[2]
    gc = jnp.cumsum(g, axis=-1)
    lower = jnp.tril(jnp.ones((L, L), dtype=bool))
    strict = jnp.tril(jnp.ones((L, L), dtype=bool), -1)
    decay = jnp.exp(jnp.where(lower, gc[..., :, None] - gc[..., None, :], -jnp.inf))
    kb = k * beta[..., None]
    lmat = jnp.where(strict, jnp.einsum('bhid,bhjd->bhij', kb, k) * decay, 0.0)
    eye = jnp.eye(L, dtype=q.dtype)
    t_inv = lax.linalg.triangular_solve(eye + lmat, jnp.broadcast_to(eye, lmat.shape),
                                        left_side=True, lower=True, unit_diagonal=True)
    u = t_inv @ (v * beta[..., None])
    w = t_inv @ (kb * jnp.exp(gc)[..., None])
    v_new = u - w @ S
    attn = jnp.einsum('bhid,bhjd->bhij', q, k) * decay
    o = (q * jnp.exp(gc)[..., None]) @ S + attn @ v_new
    g_last = gc[..., -1]
    S_new = S * jnp.exp(g_last)[..., None, None] + jnp.einsum(
        'bhld,bhle->bhde', k * jnp.exp(g_last[..., None] - gc)[..., None], v_new)
    return S_new, o

def gdn_sequence(S0, q, k, v, g, beta):
    B, H, L, _ = q.shape
    if L <= CHUNK:
        S, o = gdn_chunk(S0, q, k, v, g, beta)
        return o, S
    nc = L // CHUNK

    def to_blocks(t):
        t = t.reshape(t.shape[0], t.shape[1], nc, CHUNK, *t.shape[3:])
        return jnp.moveaxis(t, 2, 0)

    S, o = lax.scan(lambda s, c: gdn_chunk(s, *c), S0,
                    (to_blocks(q), to_blocks(k), to_blocks(v), to_blocks(g), to_blocks(beta)))
    o = jnp.moveaxis(o, 0, 2).reshape(B, H, L, GDN_DV)
    return o, S

def mixer(h, conv_l, h_l, conv_g, S_g, w_in, lru_cw, lru_cb, lru_wa, lru_ba, lru_wx, lru_bx,
          lru_lam, gdn_cw, gdn_alog, gdn_dtb, gdn_ng, w_out):
    B, L, _ = h.shape
    f32 = jnp.float32
    proj = h @ w_in
    s1 = LRU_WIDTH
    s2 = 2 * LRU_WIDTH
    s3 = s2 + GDN_CONV_CH
    s4 = s3 + GDN_V
    s5 = s4 + GDN_HEADS
    x_lru = proj[..., :s1]
    y_lru = proj[..., s1:s2]
    qkv = proj[..., s2:s3]
    z = proj[..., s3:s4]
    b_logit = proj[..., s4:s5]
    a_logit = proj[..., s5:]
    xc, new_conv_l = causal_conv(x_lru, conv_l, lru_cw)
    xc = xc + lru_cb
    hs, new_h = rglru(xc, h_l, lru_wa, lru_ba, lru_wx, lru_bx, lru_lam)
    out_a = hs * jax.nn.gelu(y_lru.astype(f32))
    qkv_c, new_conv_g = causal_conv(qkv, conv_g, gdn_cw)
    qkv_c = jax.nn.silu(qkv_c.astype(f32))

    def heads(t, d):
        return t.reshape(B, L, GDN_HEADS, d).transpose(0, 2, 1, 3)

    q = l2norm(heads(qkv_c[..., :GDN_QK], GDN_DK)) * (GDN_DK ** -0.5)
    k = l2norm(heads(qkv_c[..., GDN_QK:2 * GDN_QK], GDN_DK))
    v = heads(qkv_c[..., 2 * GDN_QK:], GDN_DV)
    beta = jax.nn.sigmoid(b_logit.astype(f32)).transpose(0, 2, 1)
    g = (-jnp.exp(gdn_alog.astype(f32)) *
         jax.nn.softplus(a_logit.astype(f32) + gdn_dtb.astype(f32))).transpose(0, 2, 1)
    o, new_S = gdn_sequence(S_g.astype(f32), q, k, v, g, beta)
    o = rmsnorm(o.transpose(0, 2, 1, 3), gdn_ng) * jax.nn.silu(
        z.astype(f32).reshape(B, L, GDN_HEADS, GDN_DV))
    mixed = jnp.concatenate([out_a, o.reshape(B, L, GDN_V)], axis=-1).astype(h.dtype)
    return mixed @ w_out, (new_conv_l, new_h, new_conv_g, new_S)

def expert_dispatch(xf, eidx, wts, w1, w3, w2):
    T, D = xf.shape
    A = T * TOP_K
    e_flat = eidx.reshape(A)
    order = jnp.argsort(e_flat)
    e_sorted = e_flat[order]
    tok_sorted = (order // TOP_K).astype(jnp.int32)
    w_sorted = wts.reshape(A)[order]
    counts = jnp.bincount(e_flat, length=N_EXPERTS)
    padded = (counts + ROW_BLOCK - 1) // ROW_BLOCK * ROW_BLOCK
    pad_end = jnp.cumsum(padded)
    pad_start = pad_end - padded
    start = jnp.cumsum(counts) - counts
    dest = pad_start[e_sorted] + jnp.arange(A) - start[e_sorted]
    n_blocks = -(-(A + N_EXPERTS * (ROW_BLOCK - 1)) // ROW_BLOCK)
    n_rows = n_blocks * ROW_BLOCK
    row_tok = jnp.zeros((n_rows,), jnp.int32).at[dest].set(tok_sorted)
    block_e = jnp.minimum(jnp.searchsorted(pad_end, jnp.arange(n_blocks) * ROW_BLOCK, side='right'),
                          N_EXPERTS - 1)
    xb = xf[row_tok].reshape(n_blocks, ROW_BLOCK, D)

    def run(args):
        e, xblk = args
        return (jax.nn.silu(xblk @ w1[e]) * (xblk @ w3[e])) @ w2[e]

    yb = lax.map(run, (block_e, xb)).reshape(n_rows, D)
    contrib = yb[dest] * w_sorted[:, None].astype(yb.dtype)
    return jnp.zeros((T, D), yb.dtype).at[tok_sorted].add(contrib)

def hier_moe(h, rg_w, rg_b, re_w, re_b, w1, w3, w2):
    B, L, D = h.shape
    xf = h.reshape(B * L, D)
    g_logit = (xf @ rg_w + rg_b).astype(jnp.float32)
    g_prob = jax.nn.softmax(g_logit, axis=-1)
    grp = jnp.argmax(g_logit, axis=-1)
    p_grp = jnp.take_along_axis(g_prob, grp[:, None], axis=-1)
    e_logit = (xf @ re_w + re_b).astype(jnp.float32).reshape(-1, N_GROUPS, EXPERTS_PER_GROUP)
    e_logit = jnp.take_along_axis(e_logit, grp[:, None, None], axis=1)[:, 0]
    top_v, top_i = lax.top_k(e_logit, TOP_K)
    wts = jax.nn.softmax(top_v, axis=-1) * p_grp
    eidx = (grp[:, None] * EXPERTS_PER_GROUP + top_i).astype(jnp.int32)
    return expert_dispatch(xf, eidx, wts, w1, w3, w2).reshape(B, L, D)

def block(x, conv_l, h_l, conv_g, S_g, ln1_g, ln2_g, w_in, lru_cw, lru_cb, lru_wa, lru_ba,
          lru_wx, lru_bx, lru_lam, gdn_cw, gdn_alog, gdn_dtb, gdn_ng, w_out,
          rg_w, rg_b, re_w, re_b, w1, w3, w2):
    mix, states = mixer(rmsnorm(x, ln1_g), conv_l, h_l, conv_g, S_g, w_in, lru_cw, lru_cb,
                        lru_wa, lru_ba, lru_wx, lru_bx, lru_lam, gdn_cw, gdn_alog, gdn_dtb,
                        gdn_ng, w_out)
    x = x + mix
    x = x + hier_moe(rmsnorm(x, ln2_g), rg_w, rg_b, re_w, re_b, w1, w3, w2)
    return x, states

def trunk(x, s_lc, s_lh, s_gc, s_gs, layer_w, final_g):
    new_lc, new_lh, new_gc, new_gs = [], [], [], []
    for l in range(DEPTH):
        x, (a, b, c, d) = block(x, s_lc[l], s_lh[l], s_gc[l], s_gs[l], *[w[l] for w in layer_w])
        new_lc.append(a.astype(s_lc.dtype))
        new_lh.append(b.astype(s_lh.dtype))
        new_gc.append(c.astype(s_gc.dtype))
        new_gs.append(d.astype(s_gs.dtype))
    return (rmsnorm(x, final_g), jnp.stack(new_lc), jnp.stack(new_lh),
            jnp.stack(new_gc), jnp.stack(new_gs))

def setup_inputs(seed: int = 0) -> dict:
    key = jax.random.key(seed)
    ks = jax.random.split(key, 32)
    f32 = jnp.float32

    def nrm(k, shape, scale):
        return jax.random.normal(k, shape, f32) * scale

    a0 = jax.random.uniform(ks[15], (DEPTH, LRU_WIDTH), f32, 0.9, 0.999) ** (1.0 / LRU_C)
    dt = jnp.exp(jax.random.uniform(ks[18], (DEPTH, GDN_HEADS), f32, math.log(1e-3), math.log(0.1)))
    return {
        'x_prompt': nrm(ks[0], (BATCH, SEQ, D_MODEL), 1.0),
        'x_sample': nrm(ks[1], (DEC_BATCH, DEC_SEQ, D_MODEL), 1.0),
        'state_lru_conv': nrm(ks[2], (DEPTH, DEC_BATCH, CONV_W - 1, LRU_WIDTH), 1.0),
        'state_lru_h': nrm(ks[3], (DEPTH, DEC_BATCH, LRU_WIDTH), 0.5),
        'state_gdn_conv': nrm(ks[4], (DEPTH, DEC_BATCH, CONV_W - 1, GDN_CONV_CH), 1.0),
        'state_gdn_S': nrm(ks[5], (DEPTH, DEC_BATCH, GDN_HEADS, GDN_DK, GDN_DV), 0.1),
        'ln1_g': 1.0 + nrm(ks[6], (DEPTH, D_MODEL), 0.02),
        'ln2_g': 1.0 + nrm(ks[7], (DEPTH, D_MODEL), 0.02),
        'w_in': nrm(ks[8], (DEPTH, D_MODEL, IN_COLS), D_MODEL ** -0.5),
        'lru_conv_w': nrm(ks[9], (DEPTH, CONV_W, LRU_WIDTH), CONV_W ** -0.5),
        'lru_conv_b': nrm(ks[10], (DEPTH, LRU_WIDTH), 0.01),
        'lru_wa': nrm(ks[11], (DEPTH, LRU_BLOCKS, LRU_BLOCK, LRU_BLOCK), LRU_BLOCK ** -0.5),
        'lru_ba': nrm(ks[12], (DEPTH, LRU_WIDTH), 0.01),
        'lru_wx': nrm(ks[13], (DEPTH, LRU_BLOCKS, LRU_BLOCK, LRU_BLOCK), LRU_BLOCK ** -0.5),
        'lru_bx': nrm(ks[14], (DEPTH, LRU_WIDTH), 0.01),
        'lru_lambda': jnp.log(a0) - jnp.log1p(-a0),
        'gdn_conv_w': nrm(ks[16], (DEPTH, CONV_W, GDN_CONV_CH), CONV_W ** -0.5),
        'gdn_a_log': jnp.log(jax.random.uniform(ks[17], (DEPTH, GDN_HEADS), f32, 1.0, 16.0)),
        'gdn_dt_bias': dt + jnp.log(-jnp.expm1(-dt)),
        'gdn_norm_g': 1.0 + nrm(ks[19], (DEPTH, GDN_DV), 0.02),
        'w_out': nrm(ks[20], (DEPTH, MIX_WIDTH, D_MODEL), MIX_WIDTH ** -0.5),
        'router_group_w': nrm(ks[21], (DEPTH, D_MODEL, N_GROUPS), D_MODEL ** -0.5),
        'router_group_b': nrm(ks[22], (DEPTH, N_GROUPS), 0.01),
        'router_expert_w': nrm(ks[23], (DEPTH, D_MODEL, N_EXPERTS), D_MODEL ** -0.5),
        'router_expert_b': nrm(ks[24], (DEPTH, N_EXPERTS), 0.01),
        'moe_w1': nrm(ks[25], (DEPTH, N_EXPERTS, D_MODEL, D_EXPERT), D_MODEL ** -0.5),
        'moe_w3': nrm(ks[26], (DEPTH, N_EXPERTS, D_MODEL, D_EXPERT), D_MODEL ** -0.5),
        'moe_w2': nrm(ks[27], (DEPTH, N_EXPERTS, D_EXPERT, D_MODEL), D_EXPERT ** -0.5),
        'final_g': 1.0 + nrm(ks[28], (D_MODEL,), 0.02),
    }

def reference(x_prompt, x_sample, state_lru_conv, state_lru_h, state_gdn_conv, state_gdn_S,
              ln1_g, ln2_g, w_in, lru_conv_w, lru_conv_b, lru_wa, lru_ba, lru_wx, lru_bx,
              lru_lambda, gdn_conv_w, gdn_a_log, gdn_dt_bias, gdn_norm_g, w_out,
              router_group_w, router_group_b, router_expert_w, router_expert_b,
              moe_w1, moe_w3, moe_w2, final_g):
    layer_w = (ln1_g, ln2_g, w_in, lru_conv_w, lru_conv_b, lru_wa, lru_ba, lru_wx, lru_bx,
               lru_lambda, gdn_conv_w, gdn_a_log, gdn_dt_bias, gdn_norm_g, w_out,
               router_group_w, router_group_b, router_expert_w, router_expert_b,
               moe_w1, moe_w3, moe_w2)
    B = x_prompt.shape[0]
    dt = x_prompt.dtype
    y_prompt, p_lc, p_lh, p_gc, p_gs = trunk(
        x_prompt,
        jnp.zeros((DEPTH, B, CONV_W - 1, LRU_WIDTH), dt),
        jnp.zeros((DEPTH, B, LRU_WIDTH), dt),
        jnp.zeros((DEPTH, B, CONV_W - 1, GDN_CONV_CH), dt),
        jnp.zeros((DEPTH, B, GDN_HEADS, GDN_DK, GDN_DV), dt),
        layer_w, final_g)
    y_sample, s_lc, s_lh, s_gc, s_gs = trunk(
        x_sample, state_lru_conv, state_lru_h, state_gdn_conv, state_gdn_S, layer_w, final_g)
    return (y_prompt, y_sample, p_lc, p_lh, p_gc, p_gs, s_lc, s_lh, s_gc, s_gs)


_drawn_inputs = setup_inputs


def setup_inputs(seed=0):
    import zlib

    import numpy as np

    out = dict(_drawn_inputs(seed))
    spreads = {}
    factors = {'lru_ba': 8.0,
     'lru_bx': 8.0,
     'gdn_norm_g': 3.015,
     'router_expert_b': 3.593,
     'final_g': 7.474,
     'router_group_b': 4.743}
    for name, (base, spread) in spreads.items():
        noise = np.random.default_rng([zlib.crc32(name.encode()), seed]).standard_normal(out[name].shape)
        drawn = base * np.exp(spread * noise) if base else spread * noise
        out[name] = __import__('jax').numpy.asarray(drawn.astype(out[name].dtype))
    for name, factor in factors.items():
        out[name] = (out[name] * factor).astype(out[name].dtype)
    return out
```

```python
import concourse.bass as bass
from concourse import mybir
from contextlib import ExitStack

FP32 = mybir.dt.float32
I32 = mybir.dt.int32
U32 = mybir.dt.uint32
ALU = mybir.AluOpType
ACT = mybir.ActivationFunctionType
AX = mybir.AxisListType

P = 128
D = 1024
KD = D // P
SEQ = 4096
SB, SL = 8, 16
GT = 4
GN = GT * P
HEADS = 4
LC = 4
QC = 12
CC = LC + QC
ZC = 4
FC = QC + ZC + LC
IN = 3080
NE, NGR, EPG = 32, 4, 8
FE = 256
EPS = 1e-6
LEVELS = [1, 2, 4, 8, 16, 32, 64]
W13, W2 = KD * 2 * FE, (FE // P) * D

COLS = {}
_n = 0
for _name, _w in (("ln1", KD), ("ln2", KD), ("cw", CC * 4), ("cb", LC), ("ba", LC), ("bx", LC), ("lam", LC),
                  ("alog", HEADS), ("dtb", HEADS), ("ng", 1), ("rb", NGR + NE), ("iota", NE),
                  ("stream", SB)):
    COLS[_name] = (_n, _n + _w)
    _n += _w
NCOL = _n
MATS = ["ident", "upto", "after", "upto_s", "after_s", "before", "ones"] + [f"level{s}" for s in LEVELS]
NMAT = len(MATS)


def tiles():
    return SEQ // P + 1


def blocks():
    n = -(-(2 * tiles() * P + NE * (P - 1)) // P)
    return n + n % 2


class Steps:

    def __init__(self, sem, names, lead=1):
        self.sem, self.names, self.next, self.lead = sem, names, 0, lead

    def did(self, name):
        assert self.names[self.next] == name, (name, self.names[self.next])
        self.next = (self.next + 1) % len(self.names)
        return self.sem, 1

    def at(self, name, turn, back=0):
        n = len(self.names)
        return self.sem, turn * n + ((self.lead - back) * n + self.names.index(name) + 1)

    def begin(self, engine):
        engine.sem_inc(self.sem, self.lead * len(self.names))


def sequence():
    out = [("Y", 0), ("X", 0), ("Y", 1), ("X", 1), ("G", 0), ("Y", 2), ("X", 2), ("R", 0), ("G", 1), ("Y", 3), ("X", 3),
           ("O", 0), ("R", 1), ("G", 2), ("Q", 0), ("O", 1), ("R", 2), ("G", 3), ("Q", 1), ("S", 0), ("O", 2), ("R", 3),
           ("Q", 2), ("S", 1), ("O", 3)]
    for m in range(3, QC):
        out += [("Q", m), ("S", m - 1)]
    return out + [("Z", 0), ("S", QC - 1), ("Z", 1), ("Z", 2), ("Z", 3), ("B", 0)]


def project_phase(nc, T, gb, const, cols):
    seq = sequence()
    chunks = [s for s in seq if s[0] in "YXQZ"]
    number = {s: n for n, s in enumerate(chunks)}
    NPB = 3
    column = {"X": 0, "Y": LC * P, "Q": 2 * LC * P, "Z": 2 * LC * P + QC * P}
    groups = SEQ // GN
    with ExitStack() as ctx:
        def sb(name, shape, dt=FP32):
            return ctx.enter_context(nc.sbuf_tensor(name, shape, dt))

        def sem(name):
            return ctx.enter_context(nc.semaphore(name))

        w_in = sb("w_in", [P, KD, IN])
        xt = sb("xt", [P, GT, D])
        hT = sb("hT", [P, KD, GN])
        junk = sb("junk", [P, D])
        win = sb("win", [P, 4, GN + 3])
        cv = sb("cv", [P, 4, GN])
        qo = sb("qo", [P, 4, GN])
        gy = sb("gy", [P, LC, GN])
        rg = sb("rg", [P, GN])
        ig = sb("ig", [P, 2, GN])
        la = sb("la", [P, 2, GN])
        th = sb("th", [P, 2, GN])
        oa = sb("oa", [P, 2, GN])
        asq = sb("asq", [P, GN])
        gates = sb("gates", [P, 2, LC, P])
        ss = sb("ss", [P, GT])
        rs = sb("rs", [P, GT])
        neghalf = sb("neghalf", [P, GT])
        eps = sb("eps", [P, GT])
        carry = sb("carry", [P, CC, 3])
        carry_s = sb("carry_s", [P, CC, SB, 3])
        hl = sb("hl", [P, LC])
        hl_s = sb("hl_s", [P, LC, SB])
        sp8 = sb("sp8", [P, LC])
        nsp8 = sb("nsp8", [P, LC])
        nea = sb("nea", [P, HEADS])
        asum = sb("asum", [P, GT, HEADS])
        aabs = sb("aabs", [P, GT, HEADS])
        aexp = sb("aexp", [P, GT, HEADS])
        alog1 = sb("alog1", [P, GT, HEADS])
        amax = sb("amax", [P, GT, HEADS])
        pT = [ctx.enter_context(nc.psum_tensor(f"pT{n}", [P, GN], FP32)) for n in range(2)]
        pP = [ctx.enter_context(nc.psum_tensor(f"pP{n}", [P, GN], FP32)) for n in range(NPB)]
        pG = [ctx.enter_context(nc.psum_tensor(f"pG{n}", [P, GN], FP32)) for n in range(2)]
        pB = ctx.enter_context(nc.psum_tensor("pB", [P, GT, 2 * HEADS], FP32))

        ident = const[:, MATS.index("ident"), :]

        def col(name, n=0, w=1):
            return cols[:, COLS[name][0] + n:COLS[name][0] + n + w]

        pe_names = [f"T{k}" for k in range(KD)] + [f"{a}{b}" for a, b in seq if a in "YXQZGB"]
        act_names = ["ss"] + [f"T{k}" for k in range(KD)] + [f"{a}{b}" for a, b in seq if a in "YXQZGRSB"]
        dve_names = ["xs"] + [{"B": "Ba"}.get(a, a) + (str(b) if a != "B" else "") for a, b in seq if a in "XGRQB"] + ["B"]
        pe_did = Steps(sem("project_pe"), pe_names)
        act_did = Steps(sem("project_act"), act_names)
        dve_did = Steps(sem("project_dve"), dve_names)
        pool_did = Steps(sem("project_pool"), ["rs"])
        weights_in = sem("weights_in")
        setup_in = sem("setup_in")
        zeroed = sem("zeroed")
        gates_zero = sem("gates_zero")
        params = sem("params")
        x_in = [sem(f"x_in{t}") for t in range(GT)]
        qo_out = [sem(f"qo_out{n}") for n in range(4)]
        oa_out = [sem(f"oa_out{n}") for n in range(2)]
        states_out = sem("states_out")
        carries_ready = sem("carries_ready")
        table_out = sem("table_out")

        block = ctx.enter_context(nc.Block())

        @block.sync
        def _(sp):
            sp.dma_start(const[:, :, :], T["mats"]).then_inc(setup_in, 16)
            sp.dma_start(cols[:, :], T["cols"]).then_inc(setup_in, 16)
            sp.dma_start(carry_s[:, :, :, :], T["conv_s"]).then_inc(setup_in, 16)
            sp.dma_start(hl_s[:, :, :], T["h_s"]).then_inc(setup_in, 16)
            sp.wait_ge(gates_zero, 1)
            for g in range(2):
                for c in range(LC):
                    for b in range(2):
                        sp.dma_start(gates[64 * b:64 * b + 64, g, c, 64 * b:64 * b + 64],
                                     T["gates"][g, 2 * c + b]).then_inc(setup_in, 16)

            def load(g, n):
                for t in range(n):
                    sp.wait_ge(*pe_did.at(f"T{KD - 1}", g, back=1))
                    sp.dma_start(xt[:, t, :], T["x"][bass.ts(g * GT + t, P), :]).then_inc(x_in[t], 16)

            load(0, GT)
            for k in range(KD):
                sp.dma_start(w_in[:, k, :], T["w_in"][:, k, :]).then_inc(weights_in, 16)
            with sp.Fori(1, groups) as g:
                load(g, GT)
            load(groups, 1)
            sp.wait_ge(zeroed, 1)
            n = T["table"].shape[0] // P
            done = 0
            while done < n:
                w = min(n - done, GN)
                sp.dma_start(T["table"][done * P:(done + w) * P, 0].rearrange("(p n) -> p n", p=P),
                             junk[:, 0:w].bitcast(I32)).then_inc(table_out, 16)
                done += w
            sp.wait_ge(table_out, 16 * -(-n // GN))
            sp.wait_ge(carries_ready, 1)
            for dst, src in (("out_conv_p", carry[:, :, :]), ("out_h_p", hl[:, :]),
                             ("out_conv_s", carry_s[:, :, :, :]), ("out_h_s", hl_s[:, :, :])):
                sp.dma_start(T[dst], src).then_inc(states_out, 16)
            sp.wait_ge(states_out, 64)

        @block.gpsimd
        def _(pool):
            pool_did.begin(pool)
            nc.gpsimd.memset(gates[:, :, :, :], 0.0).then_inc(gates_zero, 1)
            nc.gpsimd.memset(neghalf[:, :], -0.5)
            nc.gpsimd.memset(eps[:, :], EPS)
            pool.drain()

            def group(g, n):
                pool.wait_ge(*act_did.at("ss", g))
                nc.gpsimd.tensor_tensor(ss[:, 0:n], ss[:, 0:n], eps[:, 0:n], ALU.add)
                pool.drain()
                pool.wait_ge(*dve_did.at("xs", g, back=1))
                nc.gpsimd.tensor_tensor(rs[:, 0:n], ss[:, 0:n], neghalf[:, 0:n], ALU.pow).then_inc(*pool_did.did("rs"))

            with pool.Fori(0, groups) as g:
                group(g, GT)
            group(groups, 1)

        @block.tensor
        def _(pe):
            pe_did.begin(pe)
            pe.wait_ge(setup_in, 16 * (4 + 4 * LC))

            def group(g, nt):
                N = nt * P
                pe.wait_ge(*dve_did.at("xs", g))
                for k in range(KD):
                    if k < 2:
                        pe.wait_ge(*act_did.at(f"T{k + KD - 2}", g, back=1))
                    else:
                        pe.wait_ge(*act_did.at(f"T{k - 2}", g))
                    for t in range(nt):
                        ins = nc.tensor.transpose(pT[k % 2][:, t * P:(t + 1) * P], xt[:, t, k * P:(k + 1) * P], ident)
                    ins.then_inc(*pe_did.did(f"T{k}"))
                pe.wait_ge(*act_did.at(f"T{KD - 1}", g))
                for kind, m in seq:
                    if kind in "YXQZ":
                        n = number[kind, m]
                        before = chunks[n - NPB]
                        pe.wait_ge(*act_did.at(f"{before[0]}{before[1]}", g, back=int(n < NPB)))
                        c0 = column[kind] + m * P
                        for k in range(KD):
                            ins = nc.tensor.matmul(pP[n % NPB][:, 0:N], w_in[:, k, c0:c0 + P], hT[:, k, 0:N],
                                                   start=(k == 0), stop=(k == KD - 1))
                        ins.then_inc(*pe_did.did(f"{kind}{m}"))
                    elif kind == "G":
                        pe.wait_ge(*dve_did.at(f"X{m}", g))
                        pe.wait_ge(*act_did.at(f"G{(m - 1) % LC}", g, back=int(m == 0)))
                        for b in range(2):
                            ins = nc.tensor.matmul(pG[b][:, 0:N], gates[:, b, m, :], cv[:, m, 0:N], start=True, stop=True)
                        ins.then_inc(*pe_did.did(f"G{m}"))
                    elif kind == "B":
                        pe.wait_ge(*dve_did.at("B", g, back=1))
                        pe.wait_ge(*act_did.at("B0", g, back=1))
                        for t in range(nt):
                            for k in range(KD):
                                ins = nc.tensor.matmul(pB[:, t, :], hT[:, k, t * P:(t + 1) * P],
                                                       w_in[:, k, IN - 2 * HEADS:IN], start=(k == 0), stop=(k == KD - 1))
                        ins.then_inc(*pe_did.did("B0"))

            pe.wait_ge(weights_in, 16 * KD)
            with pe.Fori(0, groups) as g:
                group(g, GT)
            group(groups, 1)

        def shaped(ap, stream):
            return ap.rearrange("p (s l) -> p s l", s=SB) if stream else ap

        def window(m, off, stream):
            if stream:
                return win[:, m % 4, 0:SB * (SL + 3)].rearrange("p (s l) -> p s l", s=SB)[:, :, off:off + SL]
            return win[:, m % 4, off:off + GN]

        @block.scalar
        def _(act):
            act_did.begin(act)
            act.wait_ge(setup_in, 16 * (4 + 4 * LC))
            nc.scalar.activation(sp8[:, :], col("lam", 0, LC), ACT.Exp, scale=-1.0)
            act.drain()
            nc.scalar.activation(sp8[:, :], sp8[:, :], ACT.Ln, bias=1.0)
            nc.scalar.activation(nea[:, :], col("alog", 0, HEADS), ACT.Exp)
            act.drain()
            nc.scalar.activation(nsp8[:, :], sp8[:, :], ACT.Copy, scale=-8.0)
            nc.scalar.activation(nea[:, :], nea[:, :], ACT.Copy, scale=-1.0)
            act.drain()
            nc.scalar.activation(sp8[:, :], sp8[:, :], ACT.Copy, scale=8.0)
            act.drain()
            nc.scalar.copy(carry[:, 0, 0:1], sp8[:, 0:1]).then_inc(params, 1)

            def group(g, nt, stream):
                N = nt * P
                for t in range(nt):
                    act.drain()
                    act.wait_ge(x_in[t], (g + 1) * 16)
                    if t == 0:
                        act.wait_ge(*pool_did.at("rs", g, back=1))
                    ins = nc.scalar.activation(junk[:, :], xt[:, t, :], ACT.Square, scale=D ** -0.5,
                                               accum_out=ss[:, t:t + 1])
                ins.then_inc(*act_did.did("ss"))
                for k in range(KD):
                    act.wait_ge(*pe_did.at(f"T{k}", g))
                    nc.scalar.activation(hT[:, k, 0:N], pT[k % 2][:, 0:N], ACT.Copy, scale=col("ln1", k)
                                         ).then_inc(*act_did.did(f"T{k}"))

                def store(chunk, src, done):
                    act.dma_start(T["mixin"][:, chunk, bass.ds(g * GN, N)], src).then_inc(done, 16)

                for kind, m in seq:
                    if kind == "Y":
                        act.wait_ge(*pe_did.at(f"Y{m}", g))
                        act.wait_ge(*dve_did.at(f"R{m}", g, back=1))
                        nc.scalar.activation(gy[:, m, 0:N], pP[number[kind, m] % NPB][:, 0:N], ACT.Gelu_apprx_tanh
                                             ).then_inc(*act_did.did(f"Y{m}"))
                    elif kind in "XQ":
                        c = m if kind == "X" else LC + m
                        o = (c - 4) % CC
                        act.wait_ge(*pe_did.at(f"{kind}{m}", g))
                        act.wait_ge(*dve_did.at(f"X{o}" if o < LC else f"Q{o - LC}", g, back=int(c < 4)))
                        nc.scalar.activation(window(c, 3, stream), shaped(pP[number[kind, m] % NPB][:, 0:N], stream),
                                             ACT.Copy).then_inc(*act_did.did(f"{kind}{m}"))
                    elif kind == "G":
                        act.drain()
                        act.wait_ge(*pe_did.at(f"G{m}", g))
                        act.wait_ge(*dve_did.at(f"R{(m - 2) % LC}", g, back=int(m < 2)))
                        nc.scalar.activation(rg[:, 0:N], pG[0][:, 0:N], ACT.Sigmoid, bias=col("ba", m))
                        nc.scalar.activation(ig[:, m % 2, 0:N], pG[1][:, 0:N], ACT.Sigmoid, bias=col("bx", m))
                        act.drain()
                        nc.scalar.activation(la[:, m % 2, 0:N], rg[:, 0:N], ACT.Exp, scale=nsp8[:, m:m + 1])
                        nc.scalar.activation(th[:, m % 2, 0:N], rg[:, 0:N], ACT.Tanh, scale=sp8[:, m:m + 1]
                                             ).then_inc(*act_did.did(f"G{m}"))
                    elif kind == "R":
                        act.wait_ge(*dve_did.at(f"G{m}", g))
                        nc.scalar.activation(th[:, m % 2, 0:N], th[:, m % 2, 0:N], ACT.Sqrt
                                             ).then_inc(*act_did.did(f"R{m}"))
                    elif kind == "O":
                        act.wait_ge(*dve_did.at(f"R{m}", g))
                        store(QC + ZC + m, oa[:, m % 2, 0:N], oa_out[m % 2])
                    elif kind == "S":
                        slot = m % 4
                        act.wait_ge(*dve_did.at(f"Q{m}", g))
                        act.wait_ge(qo_out[slot], g * 64 + (m // 4 + 1) * 16)
                        nc.scalar.activation(qo[:, slot, 0:N], cv[:, slot, 0:N], ACT.Silu).then_inc(*act_did.did(f"S{m}"))
                        act.drain()
                        store(m, qo[:, slot, 0:N], qo_out[slot])
                    elif kind == "Z":
                        act.wait_ge(*pe_did.at(f"Z{m}", g))
                        act.wait_ge(qo_out[m], g * 64 + 64)
                        nc.scalar.activation(qo[:, m, 0:N], pP[number[kind, m] % NPB][:, 0:N], ACT.Silu
                                             ).then_inc(*act_did.did(f"Z{m}"))
                        act.drain()
                        store(QC + m, qo[:, m, 0:N], qo_out[m])
                    elif kind == "B":
                        act.wait_ge(*pe_did.at("B0", g))
                        act.wait_ge(*dve_did.at("Ba", g))
                        nc.scalar.activation(gb[:, bass.ds(g * GT, nt), 0:HEADS], pB[:, 0:nt, 0:HEADS], ACT.Sigmoid)
                        nc.scalar.activation(aabs[:, 0:nt], asum[:, 0:nt], ACT.Abs)
                        act.drain()
                        nc.scalar.activation(aexp[:, 0:nt], aabs[:, 0:nt], ACT.Exp, scale=-1.0)
                        act.drain()
                        nc.scalar.activation(alog1[:, 0:nt], aexp[:, 0:nt], ACT.Ln, bias=1.0).then_inc(*act_did.did("B0"))

            for s in qo_out:
                act.sem_inc(s, 16)
            with act.Fori(0, groups) as g:
                group(g, GT, False)
            group(groups, 1, True)
            for s in qo_out:
                act.wait_ge(s, 16 + 64 * (groups + 1))
            for s in oa_out:
                act.wait_ge(s, 16 + 32 * (groups + 1))

        @block.vector
        def _(dve):
            dve_did.begin(dve)
            for s in oa_out:
                dve.sem_inc(s, 16)
            dve.wait_ge(params, 1)
            nc.vector.memset(carry[:, :, :], 0.0)
            nc.vector.memset(hl[:, :], 0.0)
            dve.drain()

            def group(g, nt, stream):
                N = nt * P
                dve.wait_ge(*pool_did.at("rs", g))
                for t in range(nt):
                    ins = nc.vector.tensor_scalar(xt[:, t, :], xt[:, t, :], rs[:, t:t + 1], None, ALU.mult)
                ins.then_inc(*dve_did.did("xs"))
                kept = carry_s if stream else carry
                for kind, m in seq:
                    if kind in "XQ":
                        c = m if kind == "X" else LC + m
                        slot = c % 4
                        cw = lambda j: col("cw", 4 * c + j)
                        old = shaped(win[:, slot, 0:SB * (SL + 3)], True)[:, :, 0:3] if stream else win[:, slot, 0:3]
                        new = shaped(win[:, slot, 0:SB * (SL + 3)], True)[:, :, SL:SL + 3] if stream else win[:, slot, N:N + 3]
                        dst = shaped(cv[:, slot, 0:N], stream)
                        dve.wait_ge(*act_did.at(f"{kind}{m}", g))
                        if c >= 8:
                            dve.wait_ge(*act_did.at(f"S{c - 8}", g))
                        elif c < 4:
                            dve.wait_ge(*act_did.at(f"S{QC - 4 + c}", g, back=1))
                        else:
                            dve.wait_ge(*pe_did.at(f"G{m}", g))
                        nc.vector.tensor_copy(old, kept[:, c])
                        dve.drain()
                        if kind == "X":
                            nc.vector.tensor_scalar(dst, window(c, 0, stream), cw(0), col("cb", m), ALU.mult, ALU.add)
                        else:
                            nc.vector.tensor_scalar(dst, window(c, 0, stream), cw(0), None, ALU.mult)
                        nc.vector.tensor_copy(kept[:, c], new)
                        for j in range(1, 4):
                            dve.drain()
                            ins = nc.vector.scalar_tensor_tensor(dst, window(c, j, stream), cw(j), dst, ALU.mult, ALU.add)
                        ins.then_inc(*dve_did.did(f"{kind}{m}"))
                    elif kind == "G":
                        s = m % 2
                        dve.wait_ge(*act_did.at(f"G{m}", g))
                        nc.vector.tensor_tensor(asq[:, 0:N], la[:, s, 0:N], la[:, s, 0:N], ALU.mult)
                        nc.vector.tensor_tensor(ig[:, s, 0:N], ig[:, s, 0:N], cv[:, m, 0:N], ALU.mult)
                        dve.drain()
                        nc.vector.scalar_tensor_tensor(th[:, s, 0:N], asq[:, 0:N], 1.0, th[:, s, 0:N], ALU.add, ALU.mult
                                                       ).then_inc(*dve_did.did(f"G{m}"))
                    elif kind == "R":
                        s = m % 2
                        dve.wait_ge(*act_did.at(f"R{m}", g))
                        dve.wait_ge(oa_out[s], g * 32 + (m // 2 + 1) * 16)
                        nc.vector.tensor_tensor(ig[:, s, 0:N], ig[:, s, 0:N], th[:, s, 0:N], ALU.mult)
                        dve.drain()
                        if stream:
                            for b in range(SB):
                                r = slice(b * SL, (b + 1) * SL)
                                nc.vector.tensor_tensor_scan(oa[:, s, r], la[:, s, r], ig[:, s, r], hl_s[:, m, b:b + 1],
                                                             ALU.mult, ALU.add)
                            dve.drain()
                            nc.vector.tensor_copy(hl_s[:, m, :], shaped(oa[:, s, 0:N], True)[:, :, SL - 1])
                        else:
                            nc.vector.tensor_tensor_scan(oa[:, s, 0:N], la[:, s, 0:N], ig[:, s, 0:N], hl[:, m:m + 1],
                                                         ALU.mult, ALU.add)
                            dve.drain()
                            nc.vector.tensor_copy(hl[:, m:m + 1], oa[:, s, N - 1:N])
                        dve.drain()
                        dve.wait_ge(*act_did.at(f"Y{m}", g))
                        nc.vector.tensor_tensor(oa[:, s, 0:N], oa[:, s, 0:N], gy[:, m, 0:N], ALU.mult
                                                ).then_inc(*dve_did.did(f"R{m}"))
                    elif kind == "B":
                        dve.wait_ge(*pe_did.at("B0", g))
                        dtb = col("dtb", 0, HEADS).unsqueeze(1).to_broadcast([P, nt, HEADS])
                        neg = nea[:, :].unsqueeze(1).to_broadcast([P, nt, HEADS])
                        nc.vector.tensor_tensor(asum[:, 0:nt], pB[:, 0:nt, HEADS:], dtb, ALU.add
                                                ).then_inc(*dve_did.did("Ba"))
                        dve.drain()
                        dve.wait_ge(*act_did.at("B0", g))
                        nc.vector.scalar_tensor_tensor(amax[:, 0:nt], asum[:, 0:nt], 0.0, alog1[:, 0:nt], ALU.max, ALU.add)
                        dve.drain()
                        nc.vector.tensor_tensor(gb[:, bass.ds(g * GT, nt), HEADS:], amax[:, 0:nt], neg, ALU.mult
                                                ).then_inc(*dve_did.did("B"))

            with dve.Fori(0, groups) as g:
                group(g, GT, False)
            group(groups, 1, True)
            dve.drain()
            nc.vector.tensor_copy(rs[:, 0:1], hl[:, 0:1]).then_inc(carries_ready, 1)
            dve.wait_ge(*act_did.at("ss", groups))
            nc.vector.memset(junk[:, :], 0.0).then_inc(zeroed, 1)


MIX = """
X.sq.act X.gs.dve
Y.KS.pe Y.QS.pe Y.X.dve Y.o1.act
R.xn.dve R.h2.pool
X.stat.pe X.dec.pe X.sse.dve X.ex.act X.DT.act X.rr.pool
Y.N.pe Y.vd.dve Y.vh.act
X.kt.pe X.ktc.act X.vt.pe X.sc.dve
R.hT0.pe R.hT1.pe
Y.dS.pe Y.S.dve Y.AV.pe
X.KK.pe X.QK.pe X.vs.act X.G.dve R.hc0.dve R.hc1.dve X.B2.pool X.Z1.dve Y.o.dve X.AT.dve
R.lg.pe Y.so.act Y.ro.pool R.r0.dve R.sh.act
Y.outA0.pe X.B4.pool
X.T1.pe X.T1c.act R.r1.dve R.rx.act Y.on.dve
Y.outA1.pe X.ATm.pool
X.W2.pe X.I2.dve X.B8.pool Y.oT.pe Y.mx.dve
X.T2.pe X.Z2.pe X.T2c.act X.Z2c.act
X.W4.pe X.I4.dve R.r3.dve Y.outB0.pe X.B16.pool
X.T4.pe X.Z4.pe X.T4c.act X.Z4c.act
X.W8.pe X.I8.dve R.rk.pe Y.outB1.pe X.B32.pool
X.T8.pe X.Z8.pe X.T8c.act X.Z8c.act
X.W16.pe X.I16.dve R.off.dve Y.outB2.pe X.B64.pool
X.T16.pe X.Z16.pe X.T16c.act X.Z16c.act
X.W32.pe X.I32.dve Y.outB3.pe R.sct.pool
X.T32.pe X.Z32.pe X.T32c.act X.Z32c.act Y.x2.dve
X.W64.pe X.I64.dve Y.st.act Y.r2.pool
X.Z64.pe X.Z64c.act
""".split()
MIX = [tuple(s.split(".")) for s in MIX]
ENGINES = ("pe", "act", "dve", "pool")


def mix_phase(nc, T, gb, const, cols, eid, rank, wts, base):
    NT = tiles()
    H = HEADS
    with ExitStack() as ctx:
        def sb(name, shape, dt=FP32):
            return ctx.enter_context(nc.sbuf_tensor(name, shape, dt))

        def sem(name):
            return ctx.enter_context(nc.semaphore(name))

        w_out = sb("w_out", [P, KD, D])
        router = sb("router", [P, KD, NGR + NE])
        ln2_row = sb("ln2_row", [P, D])
        tok = sb("tok", [P, NT], I32)
        ft = [sb(f"ft{p}", [P, FC, P]) for p in range(2)]
        xr = [sb(f"xr{p}", [P, D]) for p in range(2)]
        sqb = sb("sqb", [P, 2 * H, P])
        gt = [sb(f"gt{p}", [P, 2 * H]) for p in range(2)]
        gw = sb("gw", [P, P])
        gsel = sb("gsel", [P, SB, H])
        gs = sb("gs", [P, H, P])
        DT = sb("DT", [P, H, P])
        G = sb("G", [P, H, P])
        Bs = {s: sb(f"B{s}", [P, H, P]) for s in LEVELS}
        Tm = sb("Tm", [P, H, P])
        Zm = sb("Zm", [P, H, P])
        WI = sb("WI", [P, H, P])
        Zf = [sb(f"Zf{p}", [P, H, P]) for p in range(2)]
        AT = [sb(f"AT{p}", [P, H, P]) for p in range(2)]
        ktok = [sb(f"ktok{p}", [P, H, P]) for p in range(2)]
        vs = [sb(f"vs{p}", [P, H, P]) for p in range(2)]
        sse = sb("sse", [P, 2 * H])
        rr = sb("rr", [P, 2 * H])
        ex = [sb(f"ex{p}", [P, 3 * H + SB * H]) for p in range(2)]
        sc = [sb(f"sc{p}", [P, 7, H]) for p in range(2)]
        S = sb("S", [P, H, P])
        S_s = sb("S_s", [P, SB, H, P])
        kz = sb("kz", [P, H, SB, P])
        vm = sb("vm", [P, H, P])
        xb = sb("xb", [P, H, P])
        vhat = sb("vhat", [P, H, P])
        vdec = sb("vdec", [P, H, P])
        o1 = sb("o1", [P, H, P])
        ob = sb("ob", [P, H, P])
        onb = sb("onb", [P, H, P])
        mx = sb("mx", [P, H, P])
        junk = sb("junk2", [P, D])
        so = sb("so", [P, H])
        ro = sb("ro", [P, H])
        neghalf = sb("neghalf2", [P, 2 * H])
        eps = sb("eps2", [P, 2 * H])
        x2b = sb("x2b", [P, D])
        xn = sb("xn", [P, D])
        h2b = sb("h2b", [P, D])
        s2 = sb("s2", [P, 1])
        rs2 = sb("rs2", [P, 1])
        hT = sb("hT2", [P, KD, P])
        lg = sb("lg", [P, NE])
        gpad = sb("gpad", [P, 8])
        m8 = sb("m8", [P, 8])
        i8 = sb("i8", [P, 8], U32)
        gid = sb("gid", [P, 1])
        gid8 = sb("gid8", [P, 1])
        goh = sb("goh", [P, NGR])
        esel = sb("esel", [P, EPG])
        m8e = sb("m8e", [P, 8])
        i8e = sb("i8e", [P, 8], U32)
        ief = sb("ief", [P, 2])
        e2 = sb("e2", [P, 2])
        dif = sb("dif", [P, NGR + 1])
        exd = sb("exd", [P, NGR + 1])
        sg = sb("sg", [P, 1])
        den = sb("den", [P, 1])
        w2t = sb("w2t", [P, 2])
        O0 = sb("O0", [P, NE])
        O1 = sb("O1", [P, NE])
        OO = sb("OO", [P, NE])
        rkf = sb("rkf", [P, NE])
        rjunk = sb("rjunk", [P, NE])
        r2t = sb("r2t", [P, 2])
        offs = [sb(f"offs{k}", [P, 1], I32) for k in range(2)]
        tid = sb("tid", [P, 1], I32)
        XA, XB, XC, YA, YB, YC, YD, YE = [
            ctx.enter_context(nc.psum_tensor(f"bank{n}", [P, H, P], FP32)) for n in range(8)]
        flat = lambda b: b[:, :, :].rearrange("p h n -> p (h n)")

        done = {(st, e): Steps(sem(f"mix_{st}_{e}"), [n for a, n, b in MIX if a == st and b == e], lead=2)
                for st in "XYR" for e in ENGINES if any(a == st and b == e for a, n, b in MIX)}
        owner = {n: done[st, e] for st, n, e in MIX}
        weights_in = sem("mix_weights_in")
        ft_in = [sem(f"ft_in{p}") for p in range(2)]
        xr_in = [sem(f"xr_in{p}") for p in range(2)]
        x2_out = sem("x2_out")
        h2_out = sem("h2_out")
        ids_out = sem("ids_out")
        scatters = sem("scatters")
        spread = sem("spread")
        vm_ready = sem("vm_ready")
        stream_S = sem("stream_S")
        stream_mm = sem("stream_mm")
        S_out = sem("S_out")
        S_ready = sem("S_ready")
        const2 = sem("const2")

        def at(name, t, back=0):
            return owner[name].at(name, t, back)

        def mat(name):
            return const[:, MATS.index(name), :]

        def heads(ap):
            return ap.unsqueeze(1).to_broadcast([P, H, P])

        def per_head(ap):
            return ap.unsqueeze(2).to_broadcast([P, H, P])

        def col(name, n=0, w=1):
            return cols[:, COLS[name][0] + n:COLS[name][0] + n + w]

        def program(engine, begin, x_step, y_step):
            for (st, e), d in done.items():
                if e == engine:
                    d.begin(begin)

            def run(x, y, r):
                for st, n, e in MIX:
                    tile = {"X": x, "Y": y, "R": r}[st]
                    if e == engine and tile is not None:
                        (x_step if st == "X" else y_step)(n, tile[0], tile[1], tile[2], done[st, e].did)

            last = NT - 1
            run((0, 0, False), None, None)
            run((1, 1, False), (0, 0, False), None)
            with begin.Fori(0, (last - 2) // 2) as pair:
                t = pair * 2
                run((t + 2, 0, False), (t + 1, 1, False), (t, 0, False))
                run((t + 3, 1, False), (t + 2, 0, False), (t + 1, 1, False))
            run((last, 0, True), (last - 1, 1, False), (last - 2, 0, False))
            run(None, (last, 0, True), (last - 1, 1, False))
            run(None, None, (last, 0, True))

        block = ctx.enter_context(nc.Block())

        @block.sync
        def _(sp):
            def load(t, p):
                sp.wait_ge(*at("outA1", t, 2))
                sp.wait_ge(*at("mx", t, 2))
                sp.wait_ge(*at("Z64", t, 2))
                sp.dma_start(ft[p][:, :, :], T["mixin"][:, :, bass.ts(t, P)]).then_inc(ft_in[p], 16)
                sp.wait_ge(*at("x2", t, 2))
                sp.dma_start(xr[p][:, :], T["x"][bass.ts(t, P), :]).then_inc(xr_in[p], 16)

            sp.dma_start(ft[0][:, :, :], T["mixin"][:, :, 0:P]).then_inc(ft_in[0], 16)
            sp.dma_start(xr[0][:, :], T["x"][0:P, :]).then_inc(xr_in[0], 16)
            sp.dma_start(w_out[:, :, :], T["w_out"]).then_inc(weights_in, 16)
            sp.dma_start(router[:, :, :], T["router"]).then_inc(weights_in, 16)
            sp.dma_start(ln2_row[:, :], T["ln2_row"].to_broadcast([P, D])).then_inc(weights_in, 16)
            sp.dma_start(tok[:, :], T["tokens"]).then_inc(weights_in, 16)
            sp.dma_start(S_s[:, :, :, :], T["S_s"]).then_inc(weights_in, 16)
            with sp.Fori(0, (NT - 1) // 2) as pair:
                load(pair * 2 + 1, 1)
                load(pair * 2 + 2, 0)
            sp.wait_ge(S_ready, 1)
            sp.dma_start(T["out_S_p"], S[:, :, :]).then_inc(S_out, 16)
            sp.wait_ge(S_ready, 2)
            sp.dma_start(T["out_S_s"], S_s[:, :, :, :]).then_inc(S_out, 16)
            sp.wait_ge(S_out, 32)

        def ft_turn(t, p):
            return (t - p) * 8 + 16

        @block.tensor
        def _(pe):
            ident = mat("ident")

            def x_step(n, t, p, stream, did):
                q, k, v = (lambda h: ft[p][:, h, :]), (lambda h: ft[p][:, H + h, :]), (lambda h: ft[p][:, 2 * H + h, :])
                if n == "stat":
                    pe.wait_ge(*at("I64", t, 1))
                    pe.wait_ge(*at("sq", t))
                    for c in range(2 * H):
                        nc.tensor.matmul(flat(XB)[:, c:c + P], sqb[:, c, :], mat("ones"), start=True, stop=True)
                    pe.wait_ge(*at("gs", t))
                    g = gw[:, :]
                    c = 2 * H
                    for m in ("upto_s" if stream else "upto", "after_s" if stream else "after", "ones"):
                        ins = nc.tensor.matmul(flat(XB)[:, c:c + P], mat(m), g, start=True, stop=True)
                        c += H
                    if stream:
                        ins = nc.tensor.matmul(flat(XB)[:, c:c + SB * H], mat("ones"),
                                               gsel[:, :, :].rearrange("p s h -> p (s h)"), start=True, stop=True)
                    ins.then_inc(*did(n))
                elif n == "dec":
                    pe.wait_ge(*at("Z64c", t, 1))
                    for h in range(H):
                        ins = nc.tensor.matmul(XA[:, h, :], gs[:, h, :], mat("upto_s" if stream else "upto"),
                                               start=True, stop=True)
                    ins.then_inc(*did(n))
                elif n == "kt":
                    pe.wait_ge(*at("T32c", t, 1))
                    for h in range(H):
                        ins = nc.tensor.transpose(XC[:, h, :], k(h), ident)
                    ins.then_inc(*did(n))
                elif n == "vt":
                    pe.wait_ge(*at("ex", t))
                    for h in range(H):
                        ins = nc.tensor.transpose(XB[:, h, :], v(h), ident)
                    ins.then_inc(*did(n))
                elif n == "KK":
                    pe.wait_ge(*at("DT", t))
                    for h in range(H):
                        ins = nc.tensor.matmul(XA[:, h, :], k(h), k(h), start=True, stop=True)
                    ins.then_inc(*did(n))
                elif n == "QK":
                    pe.wait_ge(*at("ktc", t))
                    for h in range(H):
                        ins = nc.tensor.matmul(XC[:, h, :], k(h), q(h), start=True, stop=True)
                    ins.then_inc(*did(n))
                elif n == "T1":
                    pe.wait_ge(*at("Z1", t))
                    for h in range(H):
                        ins = nc.tensor.transpose(XA[:, h, :], Zm[:, h, :], ident)
                    ins.then_inc(*did(n))
                elif n[0] == "W":
                    s = int(n[1:])
                    if s == 2:
                        pe.wait_ge(*at("vs", t))
                    else:
                        pe.wait_ge(*at(f"I{s // 2}", t))
                    pe.wait_ge(*at(f"B{s}", t))
                    pe.wait_ge(*at(f"T{s // 2}c", t))
                    for h in range(H):
                        ins = nc.tensor.matmul(XB[:, h, :], Bs[s][:, h, :], Tm[:, h, :], start=True, stop=True)
                    ins.then_inc(*did(n))
                elif n[0] == "T":
                    s = int(n[1:])
                    if s == 2:
                        pe.wait_ge(*at("AT", t))
                    pe.wait_ge(*at(f"I{s}", t))
                    if s > 2:
                        pe.wait_ge(*at(f"Z{s // 2}c", t))
                    for h in range(H):
                        ins = nc.tensor.matmul(XC[:, h, :], Zm[:, h, :], WI[:, h, :], start=True, stop=True)
                    ins.then_inc(*did(n))
                elif n[0] == "Z":
                    s = int(n[1:])
                    pe.wait_ge(*at(f"I{s}", t))
                    pe.wait_ge(*at("T1c" if s == 2 else f"Z{s // 2}c", t))
                    for h in range(H):
                        ins = nc.tensor.matmul(XA[:, h, :], WI[:, h, :], Zm[:, h, :], start=True, stop=True)
                    ins.then_inc(*did(n))

            def y_step(n, t, p, stream, did):
                if n in ("KS", "QS"):
                    if n == "KS":
                        pe.wait_ge(*at("off", t, 2))
                        pe.wait_ge(*at("S", t, 1))
                        pe.wait_ge(*at("Z64c", t))
                        pe.wait_ge(*at("vs", t))
                    else:
                        pe.wait_ge(*at("o", t, 1))
                    bank = YA if n == "KS" else YB
                    if stream:
                        pe.wait_ge(spread, 1 if n == "KS" else 2)
                    for h in range(H):
                        if stream:
                            for b in range(SB):
                                ins = nc.tensor.matmul(bank[:, h, :], kz[:, h, b, :], S_s[:, b, h, :],
                                                       start=(b == 0), stop=(b == SB - 1))
                        else:
                            ins = nc.tensor.matmul(bank[:, h, :], ft[p][:, (H if n == "KS" else 0) + h, :], S[:, h, :],
                                                   start=True, stop=True)
                    ins.then_inc(*did(n))
                elif n == "N":
                    pe.wait_ge(*at("X", t))
                    for h in range(H):
                        ins = nc.tensor.matmul(YA[:, h, :], Zf[p][:, h, :], xb[:, h, :], start=True, stop=True)
                    ins.then_inc(*did(n))
                elif n == "dS":
                    pe.wait_ge(*at("mx", t, 1))
                    pe.wait_ge(*at("vd", t))
                    if stream:
                        for b in range(SB):
                            pe.wait_ge(vm_ready, b + 1)
                            for h in range(H):
                                ins = nc.tensor.matmul(YC[:, h, :], ktok[p][:, h, :], vm[:, h, :], start=True, stop=True)
                            ins.then_inc(stream_mm, 1)
                            pe.wait_ge(stream_S, b + 1)
                    for h in range(H):
                        ins = nc.tensor.matmul(YC[:, h, :], ktok[p][:, h, :], vdec[:, h, :], start=True, stop=True)
                    ins.then_inc(*did(n))
                elif n == "AV":
                    pe.wait_ge(*at("o1", t))
                    pe.wait_ge(*at("vh", t))
                    pe.wait_ge(*at("ATm", t))
                    for h in range(H):
                        ins = nc.tensor.matmul(YB[:, h, :], AT[p][:, h, :], vhat[:, h, :], start=True, stop=True)
                    ins.then_inc(*did(n))
                elif n in ("outA0", "outA1"):
                    half = int(n[-1])
                    pe.wait_ge(*at("x2", t, 1))
                    pe.wait_ge(*at("r0" if half == 0 else "hc1", t, 1))
                    for c in range(LC):
                        ins = nc.tensor.matmul(flat((YD, YE)[half]), ft[p][:, QC + ZC + c, :],
                                               w_out[:, c, half * 512:half * 512 + 512], start=(c == 0), stop=False)
                    ins.then_inc(*did(n))
                elif n == "oT":
                    pe.wait_ge(*at("S", t))
                    pe.wait_ge(*at("on", t))
                    for h in range(H):
                        ins = nc.tensor.transpose(YC[:, h, :], onb[:, h, :], ident)
                    ins.then_inc(*did(n))
                elif n[:-1] == "outB":
                    pe.wait_ge(*at("mx", t))
                    half, h0 = divmod(int(n[-1]), 2)
                    for h in (2 * h0, 2 * h0 + 1):
                        ins = nc.tensor.matmul(flat((YD, YE)[half]), mx[:, h, :],
                                               w_out[:, LC + h, half * 512:half * 512 + 512], start=False, stop=(h == H - 1))
                    ins.then_inc(*did(n))
                elif n in ("hT0", "hT1"):
                    half = int(n[-1])
                    pe.wait_ge(*at("xn", t))
                    for c in range(4):
                        k = 4 * half + c
                        ins = nc.tensor.transpose((YD, YE)[half][:, c, :], xn[:, k * P:(k + 1) * P], ident)
                    ins.then_inc(*did(n))
                elif n == "lg":
                    pe.wait_ge(*at("hc1", t))
                    for k in range(KD):
                        ins = nc.tensor.matmul(flat(YD)[:, 0:NGR + NE], hT[:, k, :], router[:, k, :],
                                               start=(k == 0), stop=(k == KD - 1))
                    ins.then_inc(*did(n))
                elif n == "rk":
                    pe.wait_ge(*at("vh", t, 0 if stream else -1))
                    pe.wait_ge(*at("r3", t))
                    nc.tensor.matmul(flat(YA)[:, 0:NE], mat("before"), OO[:, :], start=True, stop=True)
                    nc.tensor.matmul(flat(YA)[:, NE:2 * NE], mat("ones"), OO[:, :], start=True, stop=True
                                     ).then_inc(*did(n))

            pe.wait_ge(weights_in, 16 * 5)
            program("pe", pe, x_step, y_step)

        @block.scalar
        def _(act):
            def x_step(n, t, p, stream, did):
                if n == "sq":
                    act.wait_ge(ft_in[p], ft_turn(t, p))
                    act.wait_ge(*at("stat", t, 1))
                    nc.scalar.activation(sqb[:, :, :], ft[p][:, 0:2 * H, :], ACT.Square).then_inc(*did(n))
                elif n == "ex":
                    act.wait_ge(*at("o", t, 2))
                    act.wait_ge(*at("sc", t, 2))
                    act.wait_ge(*at("sse", t))
                    w = 3 * H + (SB * H if stream else 0)
                    nc.scalar.activation(ex[p][:, 0:w], flat(XB)[:, 2 * H:2 * H + w], ACT.Exp).then_inc(*did(n))
                elif n == "DT":
                    act.wait_ge(*at("AT", t, 1))
                    act.wait_ge(*at("dec", t))
                    nc.scalar.activation(DT[:, :, :], XA[:, :, :], ACT.Exp).then_inc(*did(n))
                elif n == "ktc":
                    act.wait_ge(*at("dS", t, 2))
                    act.wait_ge(*at("kt", t))
                    nc.scalar.activation(ktok[p][:, :, :], XC[:, :, :], ACT.Copy).then_inc(*did(n))
                elif n == "vs":
                    act.wait_ge(*at("X", t, 2))
                    act.wait_ge(*at("vt", t))
                    act.wait_ge(*at("sc", t))
                    for h in range(H):
                        ins = nc.scalar.activation(vs[p][:, h, :], XB[:, h, :], ACT.Copy, scale=sc[p][:, 0, h:h + 1])
                    ins.then_inc(*did(n))
                elif n == "T1c":
                    act.wait_ge(*at("Z64", t, 1))
                    act.wait_ge(*at("T1", t))
                    nc.scalar.activation(Tm[:, :, :], XA[:, :, :], ACT.Copy).then_inc(*did(n))
                elif n[0] == "T":
                    act.drain()
                    act.wait_ge(*at(n[:-1], t))
                    nc.scalar.activation(Tm[:, :, :], XC[:, :, :], ACT.Copy).then_inc(*did(n))
                elif n == "Z64c":
                    act.wait_ge(*at("N", t, 2))
                    act.wait_ge(*at("Z64", t))
                    nc.scalar.activation(Zf[p][:, :, :], XA[:, :, :], ACT.Copy).then_inc(*did(n))
                elif n[0] == "Z":
                    act.drain()
                    act.wait_ge(*at(n[:-1], t))
                    nc.scalar.activation(Zm[:, :, :], XA[:, :, :], ACT.Copy).then_inc(*did(n))

            def y_step(n, t, p, stream, did):
                if n == "o1":
                    act.wait_ge(*at("o", t, 1))
                    act.wait_ge(*at("QS", t))
                    for h in range(H):
                        ins = nc.scalar.activation(o1[:, h, :], YB[:, h, :], ACT.Copy, scale=ex[p][:, h:h + 1])
                    ins.then_inc(*did(n))
                elif n == "vh":
                    act.wait_ge(*at("N", t))
                    act.wait_ge(*at("vd", t))
                    for h in range(H):
                        ins = nc.scalar.activation(vhat[:, h, :], YA[:, h, :], ACT.Copy, scale=sc[p][:, 1, h:h + 1])
                    ins.then_inc(*did(n))
                elif n == "so":
                    act.drain()
                    act.wait_ge(*at("ro", t, 1))
                    act.wait_ge(*at("o", t))
                    for h in range(H):
                        if h:
                            act.drain()
                        ins = nc.scalar.activation(junk[:, 0:P], ob[:, h, :], ACT.Square, scale=sc[p][:, 6, h:h + 1],
                                                   accum_out=so[:, h:h + 1])
                    ins.then_inc(*did(n))
                elif n == "st":
                    act.drain()
                    act.wait_ge(*at("r2", t, 1))
                    act.wait_ge(*at("x2", t))
                    act.dma_start(T["x2"][bass.ts(t, P), :], x2b[:, :]).then_inc(x2_out, 16)
                    nc.scalar.activation(junk[:, :], x2b[:, :], ACT.Square, scale=D ** -0.5, accum_out=s2[:, :]
                                         ).then_inc(*did(n))
                elif n == "sh":
                    act.wait_ge(*at("h2", t))
                    act.dma_start(T["h2"][bass.ts(t, P), :], h2b[:, :]).then_inc(h2_out, 16)
                    act.sem_inc(*did(n))
                elif n == "rx":
                    act.wait_ge(*at("r1", t))
                    nc.scalar.activation(exd[:, 0:NGR], dif[:, 0:NGR], ACT.Exp, accum_out=sg[:, :])
                    nc.scalar.activation(exd[:, NGR:], dif[:, NGR:], ACT.Exp).then_inc(*did(n))

            program("act", act, x_step, y_step)

        @block.gpsimd
        def _(pool):
            nc.gpsimd.memset(neghalf[:, :], -0.5)
            nc.gpsimd.memset(eps[:, :], EPS)
            pool.drain()

            def x_step(n, t, p, stream, did):
                if n == "rr":
                    pool.wait_ge(*at("sc", t, 1))
                    pool.wait_ge(*at("sse", t))
                    nc.gpsimd.tensor_tensor(rr[:, :], sse[:, :], neghalf[:, :], ALU.pow).then_inc(*did(n))
                elif n == "ATm":
                    pool.wait_ge(*at("AT", t))
                    nc.gpsimd.tensor_tensor(AT[p][:, :, :], AT[p][:, :, :], heads(mat("upto_s" if stream else "upto")),
                                            ALU.mult).then_inc(*did(n))
                elif n[0] == "B":
                    s = int(n[1:])
                    pool.wait_ge(*at(f"W{s}", t, 1))
                    pool.wait_ge(*at("G", t))
                    nc.gpsimd.tensor_tensor(Bs[s][:, :, :], G[:, :, :], heads(mat(f"level{s}")), ALU.mult
                                            ).then_inc(*did(n))

            def y_step(n, t, p, stream, did):
                if n == "ro":
                    pool.wait_ge(*at("on", t, 1))
                    pool.wait_ge(*at("so", t))
                    nc.gpsimd.tensor_tensor(ro[:, :], so[:, :], eps[:, 0:H], ALU.add)
                    pool.drain()
                    nc.gpsimd.tensor_tensor(ro[:, :], ro[:, :], neghalf[:, 0:H], ALU.pow)
                    pool.drain()
                    nc.gpsimd.tensor_tensor(ro[:, :], ro[:, :], sc[p][:, 3, :], ALU.mult).then_inc(*did(n))
                elif n == "r2":
                    pool.wait_ge(*at("xn", t, 1))
                    pool.wait_ge(*at("st", t))
                    nc.gpsimd.tensor_tensor(rs2[:, :], s2[:, :], eps[:, 0:1], ALU.add)
                    pool.drain()
                    nc.gpsimd.tensor_tensor(rs2[:, :], rs2[:, :], neghalf[:, 0:1], ALU.pow).then_inc(*did(n))
                elif n == "h2":
                    pool.wait_ge(h2_out, 16 * (t + 1))
                    pool.wait_ge(*at("xn", t))
                    nc.gpsimd.tensor_tensor(h2b[:, :], xn[:, :], ln2_row[:, :], ALU.mult).then_inc(*did(n))
                elif n == "sct":
                    pool.wait_ge(*at("off", t))
                    for k in range(2):
                        if k:
                            pool.wait_ge(ids_out, 32 * t + 16)
                        pool.sem_inc(scatters, 1)
                        pool.indirect_dma_start(T["table"], bass.IndirectOffsetOnAxis(ap=offs[k][:, 0:1], axis=0),
                                                tid[:, 0:1], None).then_inc(ids_out, 16)
                    pool.wait_ge(ids_out, 32 * t + 32)
                    pool.sem_inc(*did(n))

            pool.wait_ge(weights_in, 16 * 5)
            pool.sem_inc(h2_out, 16)
            program("pool", pool, x_step, y_step)
            pool.wait_ge(h2_out, 16 * (NT + 1))
            pool.wait_ge(x2_out, 16 * (NT + 1))

        @block.vector
        def _(dve):
            def x_step(n, t, p, stream, did):
                if n == "gs":
                    dve.wait_ge(*at("dec", t, 1))
                    nc.vector.tensor_copy(gt[p][:, :], gb[:, bass.ds(t, 1), :].rearrange("p a b -> p (a b)"))
                    dve.drain()
                    nc.vector.tensor_copy(gw[:, 0:H], gt[p][:, H:])
                    for h in range(H):
                        ins = nc.vector.tensor_scalar(gs[:, h, :], mat("after_s" if stream else "after"),
                                                      gt[p][:, H + h:H + h + 1], None, ALU.mult)
                    if stream:
                        ins = nc.vector.tensor_tensor(
                            gsel[:, :, :], gt[p][:, H:].unsqueeze(1).to_broadcast([P, SB, H]),
                            col("stream", 0, SB).unsqueeze(2).to_broadcast([P, SB, H]), ALU.mult)
                    ins.then_inc(*did(n))
                elif n == "sse":
                    dve.drain()
                    dve.wait_ge(*at("rr", t, 1))
                    dve.wait_ge(*at("stat", t))
                    nc.vector.tensor_scalar(sse[:, :], flat(XB)[:, 0:2 * H], EPS, None, ALU.add).then_inc(*did(n))
                elif n == "sc":
                    c = sc[p]
                    dve.wait_ge(*at("ro", t, 2))
                    dve.wait_ge(*at("vh", t, 2))
                    dve.wait_ge(*at("ex", t))
                    dve.wait_ge(*at("rr", t))
                    nc.vector.tensor_tensor(c[:, 0, :], sse[:, H:], rr[:, H:], ALU.mult)
                    nc.vector.tensor_tensor(c[:, 5, :], rr[:, H:], rr[:, H:], ALU.mult)
                    nc.vector.tensor_scalar(c[:, 2, :], ex[p][:, 0:H], -1.0, None, ALU.mult)
                    nc.vector.tensor_scalar(c[:, 3, :], rr[:, 0:H], P ** -0.5, None, ALU.mult)
                    nc.vector.tensor_scalar(c[:, 6, :], rr[:, 0:H], 1.0 / P, None, ALU.mult)
                    dve.drain()
                    nc.vector.tensor_tensor(c[:, 1, :], c[:, 5, :], gt[p][:, 0:H], ALU.mult)
                    dve.drain()
                    nc.vector.tensor_tensor(c[:, 4, :], c[:, 1, :], ex[p][:, H:2 * H], ALU.mult).then_inc(*did(n))
                elif n == "G":
                    dve.wait_ge(*at("B64", t, 1))
                    dve.wait_ge(*at("DT", t))
                    dve.wait_ge(*at("KK", t))
                    for h in range(H):
                        ins = nc.vector.scalar_tensor_tensor(G[:, h, :], XA[:, h, :], sc[p][:, 1, h:h + 1], DT[:, h, :],
                                                             ALU.mult, ALU.mult)
                    if stream:
                        dve.drain()
                        ins = nc.vector.tensor_tensor(G[:, :, :], G[:, :, :], heads(mat("upto_s")), ALU.mult)
                    ins.then_inc(*did(n))
                elif n == "AT":
                    dve.wait_ge(*at("AV", t, 2))
                    dve.wait_ge(*at("QK", t))
                    nc.vector.tensor_tensor(AT[p][:, :, :], XC[:, :, :], DT[:, :, :], ALU.mult).then_inc(*did(n))
                elif n == "Z1":
                    dve.drain()
                    dve.wait_ge(*at("Z64", t, 1))
                    nc.vector.tensor_tensor(Bs[1][:, :, :], G[:, :, :], heads(mat("level1")), ALU.mult)
                    dve.drain()
                    nc.vector.tensor_tensor(Zm[:, :, :], Bs[1][:, :, :], heads(mat("ident")), ALU.add).then_inc(*did(n))
                elif n[0] == "I":
                    dve.wait_ge(*at(f"W{n[1:]}", t))
                    nc.vector.tensor_tensor(WI[:, :, :], XB[:, :, :], heads(mat("ident")), ALU.add).then_inc(*did(n))
                if n == "I64" and stream:
                    nc.vector.memset(kz[:, :, :, :], 0.0)
                    dve.drain()
                    for b in range(SB):
                        r = slice(b * SL, (b + 1) * SL)
                        ins = nc.vector.tensor_copy(kz[:, :, b, r], ft[p][:, H:2 * H, r])
                    ins.then_inc(spread, 1)

            def y_step(n, t, p, stream, did):
                if n == "X" and stream:
                    dve.wait_ge(*at("KS", t))
                    for b in range(SB):
                        r = slice(b * SL, (b + 1) * SL)
                        ins = nc.vector.tensor_copy(kz[:, :, b, r], ft[p][:, 0:H, r])
                    ins.then_inc(spread, 1)
                if n == "X":
                    dve.wait_ge(*at("vs", t))
                    dve.wait_ge(*at("KS", t))
                    for h in range(H):
                        ins = nc.vector.scalar_tensor_tensor(xb[:, h, :], YA[:, h, :], sc[p][:, 2, h:h + 1], vs[p][:, h, :],
                                                             ALU.mult, ALU.add)
                    ins.then_inc(*did(n))
                elif n == "vd":
                    dve.wait_ge(*at("N", t))
                    nc.vector.tensor_tensor(vdec[:, :, :], YA[:, :, :], per_head(sc[p][:, 4, :]), ALU.mult
                                            ).then_inc(*did(n))
                    if stream:
                        for b in range(SB):
                            if b == 0:
                                dve.drain()
                            else:
                                dve.wait_ge(stream_mm, b)
                            nc.vector.tensor_scalar(vm[:, :, :], vdec[:, :, :], col("stream", b), None, ALU.mult
                                                    ).then_inc(vm_ready, 1)
                            dve.wait_ge(stream_mm, b + 1)
                            for h in range(H):
                                e = 3 * H + b * H + h
                                ins = nc.vector.scalar_tensor_tensor(S_s[:, b, h, :], S_s[:, b, h, :], ex[p][:, e:e + 1],
                                                                     YC[:, h, :], ALU.mult, ALU.add)
                            ins.then_inc(stream_S, 1)
                elif n == "S":
                    dve.wait_ge(*at("dS", t))
                    if stream:
                        nc.vector.tensor_copy(vm[:, 0, 0:1], YC[:, 0, 0:1]).then_inc(*did(n))
                    else:
                        for h in range(H):
                            ins = nc.vector.scalar_tensor_tensor(S[:, h, :], S[:, h, :], ex[p][:, 2 * H + h:2 * H + h + 1],
                                                                 YC[:, h, :], ALU.mult, ALU.add)
                        ins.then_inc(*did(n))
                elif n == "o":
                    dve.wait_ge(*at("so", t, 1))
                    dve.wait_ge(*at("o1", t))
                    dve.wait_ge(*at("AV", t))
                    nc.vector.tensor_tensor(ob[:, :, :], YB[:, :, :], o1[:, :, :], ALU.add).then_inc(*did(n))
                elif n == "on":
                    dve.wait_ge(*at("oT", t, 1))
                    dve.wait_ge(*at("ro", t))
                    nc.vector.tensor_tensor(onb[:, :, :], ob[:, :, :], per_head(ro[:, :]), ALU.mult).then_inc(*did(n))
                elif n == "mx":
                    dve.wait_ge(*at("oT", t))
                    nc.vector.scalar_tensor_tensor(mx[:, :, :], YC[:, :, :], col("ng"), ft[p][:, QC:QC + ZC, :],
                                                   ALU.mult, ALU.mult).then_inc(*did(n))
                elif n == "x2":
                    dve.wait_ge(xr_in[p], ft_turn(t, p))
                    dve.wait_ge(x2_out, 16 * (t + 1))
                    dve.wait_ge(*at("st", t, 1))
                    dve.wait_ge(*at("outB3", t))
                    nc.vector.tensor_tensor(x2b[:, 0:512], flat(YD), xr[p][:, 0:512], ALU.add)
                    nc.vector.tensor_tensor(x2b[:, 512:], flat(YE), xr[p][:, 512:], ALU.add).then_inc(*did(n))
                elif n == "xn":
                    dve.wait_ge(*at("h2", t, 1))
                    dve.wait_ge(*at("hT1", t, 1))
                    dve.wait_ge(*at("r2", t))
                    nc.vector.tensor_scalar(xn[:, :], x2b[:, :], rs2[:, 0:1], None, ALU.mult).then_inc(*did(n))
                elif n in ("hc0", "hc1"):
                    half = int(n[-1])
                    dve.wait_ge(*at(f"hT{half}", t))
                    nc.vector.tensor_tensor(hT[:, 4 * half:4 * half + 4, :], (YD, YE)[half][:, :, :],
                                            per_head(col("ln2", 4 * half, 4)), ALU.mult).then_inc(*did(n))
                elif n == "r0":
                    dve.drain()
                    dve.wait_ge(*at("lg", t))
                    nc.vector.tensor_tensor(gpad[:, 0:NGR], flat(YD)[:, 0:NGR], col("rb", 0, NGR), ALU.add)
                    nc.vector.tensor_tensor(lg[:, :], flat(YD)[:, NGR:NGR + NE], col("rb", NGR, NE), ALU.add
                                            ).then_inc(*did(n))
                elif n == "r1":
                    dve.drain()
                    nc.vector.max(m8[:, :], gpad[:, :])
                    dve.drain()
                    nc.vector.max_index(i8[:, :], m8[:, :], gpad[:, :])
                    dve.drain()
                    nc.vector.tensor_copy(gid[:, :], i8[:, 0:1])
                    dve.drain()
                    nc.vector.tensor_scalar(goh[:, :], col("iota", 0, NGR), gid[:, 0:1], None, ALU.is_equal)
                    nc.vector.tensor_scalar(gid8[:, :], gid[:, :], float(EPG), None, ALU.mult)
                    dve.drain()
                    nc.vector.tensor_scalar(esel[:, :], lg[:, 0:EPG], goh[:, 0:1], None, ALU.mult)
                    for g in range(1, NGR):
                        dve.drain()
                        nc.vector.scalar_tensor_tensor(esel[:, :], lg[:, g * EPG:(g + 1) * EPG], goh[:, g:g + 1], esel[:, :],
                                                       ALU.mult, ALU.add)
                    dve.drain()
                    nc.vector.max(m8e[:, :], esel[:, :])
                    dve.drain()
                    nc.vector.max_index(i8e[:, :], m8e[:, :], esel[:, :])
                    dve.wait_ge(*at("rx", t, 1))
                    nc.vector.tensor_scalar(dif[:, 0:NGR], gpad[:, 0:NGR], m8[:, 0:1], None, ALU.subtract)
                    nc.vector.tensor_tensor(dif[:, NGR:], m8e[:, 1:2], m8e[:, 0:1], ALU.subtract).then_inc(*did(n))
                elif n == "r3":
                    dve.wait_ge(*at("rx", t))
                    nc.vector.scalar_tensor_tensor(den[:, :], exd[:, NGR:], 1.0, sg[:, :], ALU.add, ALU.mult)
                    nc.vector.tensor_copy(ief[:, :], i8e[:, 0:2])
                    dve.drain()
                    nc.vector.reciprocal(w2t[:, 0:1], den[:, :])
                    nc.vector.tensor_scalar(e2[:, :], ief[:, :], gid8[:, 0:1], None, ALU.add)
                    dve.drain()
                    nc.vector.tensor_tensor(w2t[:, 1:2], w2t[:, 0:1], exd[:, NGR:], ALU.mult)
                    dve.wait_ge(*at("rk", t, 1))
                    nc.vector.tensor_scalar(O0[:, :], col("iota", 0, NE), e2[:, 0:1], None, ALU.is_equal)
                    nc.vector.tensor_scalar(O1[:, :], col("iota", 0, NE), e2[:, 1:2], None, ALU.is_equal)
                    dve.drain()
                    nc.vector.tensor_tensor(OO[:, :], O0[:, :], O1[:, :], ALU.add).then_inc(*did(n))
                    nc.vector.tensor_copy(wts[:, bass.ds(t, 1), :].rearrange("p a b -> p (a b)"), w2t[:, :])
                    nc.vector.tensor_copy(eid[:, bass.ds(t, 1), :].rearrange("p a b -> p (a b)"), e2[:, :])
                elif n == "off":
                    dve.wait_ge(*at("sct", t, 1))
                    dve.wait_ge(*at("rk", t))
                    old, new = base[:, 0, :], base[:, 1, :]
                    nc.vector.tensor_tensor(rkf[:, :], flat(YA)[:, 0:NE], old, ALU.add)
                    nc.vector.tensor_tensor(new, flat(YA)[:, NE:2 * NE], old, ALU.add)
                    nc.vector.tensor_copy(tid[:, :], tok[:, bass.ds(t, 1)])
                    dve.drain()
                    nc.vector.tensor_copy(old, new)
                    nc.vector.scalar_tensor_tensor(rjunk[:, :], rkf[:, :], 1.0, O0[:, :], ALU.mult, ALU.mult,
                                                   accum_out=r2t[:, 0:1])
                    dve.drain()
                    nc.vector.scalar_tensor_tensor(rjunk[:, :], rkf[:, :], 1.0, O1[:, :], ALU.mult, ALU.mult,
                                                   accum_out=r2t[:, 1:2])
                    dve.drain()
                    nc.vector.tensor_copy(rank[:, bass.ds(t, 1), :].rearrange("p a b -> p (a b)"), r2t[:, :])
                    for k in range(2):
                        ins = nc.vector.scalar_tensor_tensor(offs[k][:, :], e2[:, k:k + 1], float(NT * P), r2t[:, k:k + 1],
                                                             ALU.mult, ALU.add)
                    ins.then_inc(*did(n))

            nc.vector.memset(S[:, :, :], 0.0)
            nc.vector.memset(gw[:, :], 0.0)
            nc.vector.memset(base[:, :, :], 0.0)
            nc.vector.memset(gpad[:, :], -1e30)
            dve.sem_inc(x2_out, 16)
            dve.drain()
            program("dve", dve, x_step, y_step)
            dve.drain()
            nc.vector.tensor_copy(rjunk[:, 0:1], S[:, 0, 0:1]).then_inc(S_ready, 2)


EXPERTS = """
M.up.pe M.silu.act M.mul.dve
O.gT.pe O.gTc.act
T.T0.pe T.T1.pe T.T0c.act T.T1c.dve
O.d0.pe O.d1.pe O.d0c.act O.d1c.dve O.st.act
""".split()
EXPERTS = [tuple(s.split(".")) for s in EXPERTS]


def routing_phase(nc, T, cols, eid, rank, base, dest, tabs):
    NT, NB = tiles(), blocks()
    with ExitStack() as ctx:
        def sb(name, shape, dt=FP32):
            return ctx.enter_context(nc.sbuf_tensor(name, shape, dt))

        cnt = sb("cnt", [P, NE], I32)
        nb = sb("nb", [P, NE])
        ones = sb("ones_r", [P, NE])
        end = sb("end", [P, NE])
        start = sb("start", [P, NE])
        hot = sb("hot", [P, 2 * NT, NE])
        first = sb("first", [P, 2 * NT])
        bi = sb("bi", [1, NB])
        past = sb("past", [1, NB, NE])
        be = sb("be", [1, NB])
        bs = sb("bs", [1, NB])
        lst = sb("lst", [1, NB])
        valid = sb("valid", [1, NB])
        bi_in = ctx.enter_context(nc.semaphore("bi_in"))
        block = ctx.enter_context(nc.Block())

        @block.sync
        def _(sp):
            sp.dma_start(bi[:, :], T["block_iota"]).then_inc(bi_in, 16)

        @block.vector
        def _(dve):
            v = nc.vector
            iota = cols[:, COLS["iota"][0]:COLS["iota"][1]]
            v.tensor_scalar(cnt[:, :], base[:, 0, :], float(P - 1), None, ALU.add)
            v.memset(ones[:, :], 1.0)
            dve.drain()
            v.tensor_scalar(cnt[:, :], cnt[:, :], 7, None, ALU.logical_shift_right)
            dve.drain()
            v.tensor_copy(nb[:, :], cnt[:, :])
            dve.drain()
            v.tensor_tensor_scan(end[:, :], ones[:, :], nb[:, :], 0.0, ALU.mult, ALU.add)
            dve.drain()
            v.tensor_tensor(start[:, :], end[:, :], nb[:, :], ALU.subtract)
            dve.drain()
            v.tensor_scalar(start[:, :], start[:, :], float(P), None, ALU.mult)
            v.tensor_tensor(hot[:, :, :], eid[:, :, :].rearrange("p t k -> p (t k)").unsqueeze(2).to_broadcast([P, 2 * NT, NE]),
                            iota.unsqueeze(1).to_broadcast([P, 2 * NT, NE]), ALU.is_equal)
            dve.drain()
            v.tensor_tensor(hot[:, :, :], hot[:, :, :], start[:, :].unsqueeze(1).to_broadcast([P, 2 * NT, NE]), ALU.mult)
            dve.drain()
            v.reduce_sum(first[:, :], hot[:, :, :], AX.X)
            dve.drain()
            v.tensor_tensor(dest[:, :], first[:, :], rank[:, :, :].rearrange("p t k -> p (t k)"), ALU.add)
            dve.wait_ge(bi_in, 16)
            v.tensor_tensor(past[:, :, :], bi[:, :].unsqueeze(2).to_broadcast([1, NB, NE]),
                            end[0:1, :].unsqueeze(1).to_broadcast([1, NB, NE]), ALU.is_ge)
            dve.drain()
            v.reduce_sum(be[:, :], past[:, :, :], AX.X)
            dve.drain()
            v.tensor_tensor(past[:, :, :], past[:, :, :], nb[0:1, :].unsqueeze(1).to_broadcast([1, NB, NE]), ALU.mult)
            v.tensor_scalar(be[:, :], be[:, :], float(NE - 1), None, ALU.min)
            dve.drain()
            v.reduce_sum(bs[:, :], past[:, :, :], AX.X)
            v.tensor_scalar(valid[:, :], bi[:, :], end[0:1, NE - 1:NE], None, ALU.is_lt)
            v.tensor_copy(tabs["expert"][:, :], be[:, :])
            v.tensor_copy(tabs["end"][:, :], end[0:1, :])
            dve.drain()
            v.tensor_tensor(bs[:, :], bi[:, :], bs[:, :], ALU.subtract)
            v.tensor_scalar(lst[:, :], be[:, :], float(NT * P), -float(NE * NT * P), ALU.mult, ALU.add)
            v.tensor_scalar(tabs["slot"][:, :], tabs["expert"][:, :], 1, None, ALU.bitwise_and)
            dve.drain()
            v.scalar_tensor_tensor(lst[:, :], bs[:, :], float(P), lst[:, :], ALU.mult, ALU.add)
            dve.drain()
            v.tensor_tensor(lst[:, :], lst[:, :], valid[:, :], ALU.mult)
            dve.drain()
            v.tensor_scalar(tabs["list"][:, :], lst[:, :], float(NE * NT * P), None, ALU.add)


def experts_phase(nc, T, const, tabs):
    NT, NB = tiles(), blocks()
    with ExitStack() as ctx:
        def sb(name, shape, dt=FP32):
            return ctx.enter_context(nc.sbuf_tensor(name, shape, dt))

        def sem(name):
            return ctx.enter_context(nc.semaphore(name))

        w13 = sb("w13", [P, 2, W13])
        w2 = sb("w2", [P, 2, W2])
        idx = [sb(f"idx{p}", [P, 1], I32) for p in range(2)]
        xb = [sb(f"rows{p}", [P, D]) for p in range(2)]
        xT = [sb(f"rowsT{p}", [P, KD, P]) for p in range(2)]
        sil = [sb(f"sil{p}", [P, FE]) for p in range(2)]
        gu = [sb(f"gu{p}", [P, FE]) for p in range(2)]
        guT = [sb(f"guT{p}", [P, FE // P, P]) for p in range(2)]
        yb = [sb(f"yb{p}", [P, D]) for p in range(2)]
        TA, TB, M0, M1, GB, OA, OB = [ctx.enter_context(nc.psum_tensor(f"ebank{n}", [P, 512], FP32)) for n in range(7)]

        done = {(st, e): Steps(sem(f"experts_{st}_{e}"), [n for a, n, b in EXPERTS if a == st and b == e], lead=2)
                for st in "TMO" for e in ("pe", "act", "dve") if any(a == st and b == e for a, n, b in EXPERTS)}
        owner = {n: done[st, e] for st, n, e in EXPERTS}
        loaded = [sem(f"expert_loaded{p}") for p in range(2)]
        ready = sem("expert_ready")
        idx_in = [sem(f"idx_in{p}") for p in range(2)]
        rows_in = [sem(f"rows_in{p}") for p in range(2)]
        y_out = [sem(f"y_out{p}") for p in range(2)]
        gathers = sem("gathers")

        def at(name, t, back=0):
            return owner[name].at(name, t, back)

        def turn(b, p):
            return (b - p) * 8 + 16

        def program(engine, begin, step):
            for key, d in done.items():
                if key[1] == engine:
                    d.begin(begin)

            def run(bt, bm, bo):
                for st, n, e in EXPERTS:
                    b = {"T": bt, "M": bm, "O": bo}[st]
                    if e == engine and b is not None:
                        step(n, b[0], b[1], done[st, e].did)

            run((0, 0), None, None)
            run((1, 1), (0, 0), None)
            with begin.Fori(0, (NB - 2) // 2) as pair:
                b = pair * 2
                run((b + 2, 0), (b + 1, 1), (b, 0))
                run((b + 3, 1), (b + 2, 0), (b + 1, 1))
            run(None, (NB - 1, 1), (NB - 2, 0))
            run(None, None, (NB - 1, 1))

        block = ctx.enter_context(nc.Block())

        @block.sync
        def _(sp):
            def load(e, p):
                sp.dma_start(w13[:, p, :], T["w13"][bass.ds(e, 1)].rearrange("a p n -> p (a n)")).then_inc(loaded[p], 16)
                sp.dma_start(w2[:, p, :], T["w2"][bass.ds(e, 1)].rearrange("a p n -> p (a n)")).then_inc(loaded[p], 16)
                sp.wait_ge(loaded[p], (e - p) * 16 + 32)
                sp.sem_inc(ready, 1)

            load(0, 0)
            load(1, 1)
            with sp.Fori(0, (NE - 2) // 2) as pair:
                for p in range(2):
                    end = sp.value_load(tabs["end"][0:1, bass.ds(pair * 2 + p, 1)], min_val=0, max_val=NB)
                    sem_, value = at("d1", end, 1)
                    sp.wait_ge(sem_, value)
                    load(pair * 2 + (2 + p), p)

        @block.gpsimd
        def _(pool):
            def fetch(b, p):
                where = pool.value_load(tabs["list"][0:1, bass.ds(b, 1)], min_val=0, max_val=NE * NT * P)
                pool.wait_ge(*at("T1", b, 2))
                pool.dma_start(idx[p][:, :], T["table"][bass.ds(where, P), :]).then_inc(idx_in[p], 16)
                pool.wait_ge(idx_in[p], turn(b, p))
                pool.sem_inc(gathers, 1)
                pool.indirect_dma_start(xb[p][:, :], None, T["h2"], bass.IndirectOffsetOnAxis(ap=idx[p][:, 0:1], axis=0)
                                        ).then_inc(rows_in[p], 16)

            with pool.Fori(0, NB // 2) as pair:
                fetch(pair * 2, 0)
                fetch(pair * 2 + 1, 1)

        @block.tensor
        def _(pe):
            ident = const[:, MATS.index("ident"), :]

            def step(n, b, p, did):
                if n in ("T0", "T1"):
                    h = int(n[1])
                    bank = (TA, TB)[h]
                    pe.wait_ge(*at("T0c" if h == 0 else "T1c", b, 1))
                    pe.wait_ge(rows_in[p], turn(b, p))
                    for k in range(4):
                        c = 4 * h + k
                        ins = nc.tensor.transpose(bank[:, k * P:(k + 1) * P], xb[p][:, c * P:(c + 1) * P], ident)
                    ins.then_inc(*did(n))
                elif n == "up":
                    e = pe.value_load(tabs["expert"][0:1, bass.ds(b, 1)], min_val=0, max_val=NE - 1)
                    s = pe.value_load(tabs["slot"][0:1, bass.ds(b, 1)], min_val=0, max_val=1)
                    pe.wait_ge(ready, e + 1)
                    pe.wait_ge(*at("mul", b, 2))
                    pe.wait_ge(*at("T0c", b))
                    pe.wait_ge(*at("T1c", b))
                    for k in range(KD):
                        ins = nc.tensor.matmul((M0, M1)[p][:, :], xT[p][:, k, :],
                                               w13[:, bass.ds(s, 1), k * 512:(k + 1) * 512].rearrange("p a n -> p (a n)"),
                                               start=(k == 0), stop=(k == KD - 1))
                    ins.then_inc(*did(n))
                elif n == "gT":
                    pe.wait_ge(*at("gTc", b, 1))
                    pe.wait_ge(*at("mul", b))
                    for k in range(FE // P):
                        ins = nc.tensor.transpose(GB[:, k * P:(k + 1) * P], gu[p][:, k * P:(k + 1) * P], ident)
                    ins.then_inc(*did(n))
                elif n in ("d0", "d1"):
                    h = int(n[1])
                    if h == 0:
                        pe_slot[0] = pe.value_load(tabs["slot"][0:1, bass.ds(b, 1)], min_val=0, max_val=1)
                    pe.wait_ge(*at("d0c" if h == 0 else "d1c", b, 1))
                    pe.wait_ge(*at("gTc", b))
                    for k in range(FE // P):
                        w = w2[:, bass.ds(pe_slot[0], 1), k * D + h * 512:k * D + h * 512 + 512]
                        ins = nc.tensor.matmul((OA, OB)[h][:, :], guT[p][:, k, :], w.rearrange("p a n -> p (a n)"),
                                               start=(k == 0), stop=(k == FE // P - 1))
                    ins.then_inc(*did(n))

            pe_slot = [None]
            program("pe", pe, step)

        @block.scalar
        def _(act):
            def step(n, b, p, did):
                if n == "T0c":
                    act.wait_ge(*at("up", b, 2))
                    act.wait_ge(*at("T0", b))
                    nc.scalar.activation(xT[p][:, 0:4, :].rearrange("p k n -> p (k n)"), TA[:, :], ACT.Copy).then_inc(*did(n))
                elif n == "silu":
                    act.wait_ge(*at("mul", b, 2))
                    act.wait_ge(*at("up", b))
                    nc.scalar.activation(sil[p][:, :], (M0, M1)[p][:, 0:FE], ACT.Silu).then_inc(*did(n))
                elif n == "gTc":
                    act.wait_ge(*at("d1", b, 2))
                    act.wait_ge(*at("gT", b))
                    nc.scalar.activation(guT[p][:, :, :].rearrange("p k n -> p (k n)"), GB[:, 0:FE], ACT.Copy
                                         ).then_inc(*did(n))
                elif n == "d0c":
                    act.wait_ge(y_out[p], turn(b, p))
                    act.wait_ge(*at("d0", b))
                    nc.scalar.activation(yb[p][:, 0:512], OA[:, :], ACT.Copy).then_inc(*did(n))
                elif n == "st":
                    act.wait_ge(*at("d0c", b))
                    act.wait_ge(*at("d1c", b))
                    act.dma_start(T["y"][bass.ts(b, P), :], yb[p][:, :]).then_inc(y_out[p], 16)
                    act.sem_inc(*did(n))

            for p in range(2):
                act.sem_inc(y_out[p], 16)
            program("act", act, step)
            for p in range(2):
                act.wait_ge(y_out[p], NB // 2 * 16 + 16)

        @block.vector
        def _(dve):
            def step(n, b, p, did):
                if n == "T1c":
                    dve.wait_ge(*at("up", b, 2))
                    dve.wait_ge(*at("T1", b))
                    nc.vector.tensor_copy(xT[p][:, 4:8, :].rearrange("p k n -> p (k n)"), TB[:, :]).then_inc(*did(n))
                elif n == "mul":
                    dve.wait_ge(*at("gT", b, 2))
                    dve.wait_ge(*at("silu", b))
                    nc.vector.tensor_tensor(gu[p][:, :], (M0, M1)[p][:, FE:2 * FE], sil[p][:, :], ALU.mult
                                            ).then_inc(*did(n))
                elif n == "d1c":
                    dve.wait_ge(y_out[p], turn(b, p))
                    dve.wait_ge(*at("d1", b))
                    nc.vector.tensor_copy(yb[p][:, 512:], OB[:, :]).then_inc(*did(n))

            program("dve", dve, step)


def combine_phase(nc, T, dest, wts):
    NT = tiles()
    with ExitStack() as ctx:
        def sb(name, shape, dt=FP32):
            return ctx.enter_context(nc.sbuf_tensor(name, shape, dt))

        def sem(name):
            return ctx.enter_context(nc.semaphore(name))

        NS = 2
        final_row = sb("final_row", [P, D])
        at_row = [[sb(f"at_row{s}_{k}", [P, 1], I32) for k in range(2)] for s in range(NS)]
        yr = [[sb(f"yr{s}_{k}", [P, D]) for k in range(2)] for s in range(NS)]
        xx = [sb(f"xx{s}", [P, D]) for s in range(NS)]
        yo = [sb(f"yo{s}", [P, D]) for s in range(NS)]
        junk = sb("junk3", [P, D])
        ss = [sb(f"ss3_{s}", [P, 1]) for s in range(NS)]
        rs = [sb(f"rs3_{s}", [P, 1]) for s in range(NS)]
        neghalf = sb("neghalf3", [P, 1])
        eps = sb("eps3", [P, 1])
        row_in = sem("row_in")
        x_in = [sem(f"x2_in{s}") for s in range(NS)]
        y_in = [sem(f"y_in{s}") for s in range(NS)]
        out_done = [sem(f"out_done{s}") for s in range(NS)]
        gathers = sem("y_gathers")
        names = {"act": ["ss"], "pool": ["rs"], "dve": ["sum", "out"], "rows": ["rows"]}
        done = {e: Steps(sem(f"combine_{e}"), n, lead=2) for e, n in names.items()}
        block = ctx.enter_context(nc.Block())

        def at(e, n, t, back=0):
            return done[e].at(n, t, back)

        def turn(t, p):
            return (t - p) * 8 + 16

        def every(engine, step):
            with engine.Fori(0, NT // 2) as pair:
                step(pair * 2, 0)
                step(pair * 2 + 1, 1)
            step(NT - 1, 0)

        @block.sync
        def _(sp):
            sp.dma_start(final_row[:, :], T["final_row"].to_broadcast([P, D])).then_inc(row_in, 16)

            def step(t, p):
                sp.wait_ge(*at("dve", "sum", t, 2))
                sp.dma_start(xx[p][:, :], T["x2"][bass.ts(t, P), :]).then_inc(x_in[p], 16)

            every(sp, step)

        @block.gpsimd
        def _(pool):
            done["pool"].begin(pool)
            nc.gpsimd.memset(neghalf[:, :], -0.5)
            nc.gpsimd.memset(eps[:, :], EPS)
            pool.drain()

            def gather(t, p):
                pool.wait_ge(*at("dve", "sum", t, 2))
                pool.wait_ge(*at("rows", "rows", t))
                pool.sem_inc(gathers, 1)
                for k in range(2):
                    pool.indirect_dma_start(yr[p][k][:, :], None, T["y"],
                                            bass.IndirectOffsetOnAxis(ap=at_row[p][k][:, 0:1], axis=0)).then_inc(y_in[p], 16)

            def scale(t, p):
                pool.wait_ge(*at("dve", "out", t, 2))
                pool.wait_ge(*at("act", "ss", t))
                nc.gpsimd.tensor_tensor(rs[p][:, :], ss[p][:, :], eps[:, :], ALU.add)
                pool.drain()
                nc.gpsimd.tensor_tensor(rs[p][:, :], rs[p][:, :], neghalf[:, :], ALU.pow).then_inc(*done["pool"].did("rs"))

            gather(0, 0)
            with pool.Fori(0, NT // 2) as pair:
                gather(pair * 2 + 1, 1)
                scale(pair * 2, 0)
                gather(pair * 2 + 2, 0)
                scale(pair * 2 + 1, 1)
            scale(NT - 1, 0)

        @block.scalar
        def _(act):
            done["act"].begin(act)

            def step(t, p):
                act.drain()
                act.wait_ge(*at("pool", "rs", t, 2))
                act.wait_ge(*at("dve", "sum", t))
                nc.scalar.activation(junk[:, :], yo[p][:, :], ACT.Square, scale=D ** -0.5, accum_out=ss[p][:, :]
                                     ).then_inc(*done["act"].did("ss"))
                act.wait_ge(*at("dve", "out", t))
                act.dma_start(T["out_y"][bass.ts(t, P), :], yo[p][:, :]).then_inc(out_done[p], 16)

            for p in range(NS):
                act.sem_inc(out_done[p], 16)
            every(act, step)
            act.wait_ge(out_done[0], 16 * ((NT + 1) // 2 + 1))
            act.wait_ge(out_done[1], 16 * (NT // 2 + 1))

        @block.vector
        def _(dve):
            done["dve"].begin(dve)
            done["rows"].begin(dve)
            did = done["dve"].did

            def rows(t, p):
                for k in range(2):
                    ins = nc.vector.tensor_copy(at_row[p][k][:, :], dest[:, bass.ds(t * 2 + k, 1)])
                ins.then_inc(*done["rows"].did("rows"))

            def weight(t, k):
                return wts[:, bass.ds(t, 1), k:k + 1].rearrange("p a b -> p (a b)")

            def step(t, p):
                dve.wait_ge(out_done[p], turn(t, p))
                dve.wait_ge(x_in[p], turn(t, p))
                dve.wait_ge(y_in[p], (t - p) * 16 + 32)
                nc.vector.scalar_tensor_tensor(yo[p][:, :], yr[p][0][:, :], weight(t, 0), xx[p][:, :], ALU.mult, ALU.add)
                dve.drain()
                nc.vector.scalar_tensor_tensor(yo[p][:, :], yr[p][1][:, :], weight(t, 1), yo[p][:, :], ALU.mult, ALU.add
                                               ).then_inc(*did("sum"))
                dve.wait_ge(*at("pool", "rs", t))
                nc.vector.scalar_tensor_tensor(yo[p][:, :], yo[p][:, :], rs[p][:, 0:1], final_row[:, :], ALU.mult, ALU.mult
                                               ).then_inc(*did("out"))

            dve.wait_ge(row_in, 16)
            rows(0, 0)
            with dve.Fori(0, NT // 2) as pair:
                rows(pair * 2 + 1, 1)
                step(pair * 2, 0)
                rows(pair * 2 + 2, 0)
                step(pair * 2 + 1, 1)
            step(NT - 1, 0)


def build(nc, T):
    with ExitStack() as ctx:
        gb = ctx.enter_context(nc.sbuf_tensor("gb", [P, tiles(), 2 * HEADS], FP32))
        const = ctx.enter_context(nc.sbuf_tensor("const", [P, NMAT, P], FP32))
        cols = ctx.enter_context(nc.sbuf_tensor("cols_sb", [P, NCOL], FP32))
        eid = ctx.enter_context(nc.sbuf_tensor("eid", [P, tiles(), 2], FP32))
        rank = ctx.enter_context(nc.sbuf_tensor("rank", [P, tiles(), 2], FP32))
        wts = ctx.enter_context(nc.sbuf_tensor("wts", [P, tiles(), 2], FP32))
        base = ctx.enter_context(nc.sbuf_tensor("base", [P, 2, NE], FP32))
        dest = ctx.enter_context(nc.sbuf_tensor("dest", [P, 2 * tiles()], I32))
        tabs = {n: ctx.enter_context(nc.sbuf_tensor("tab_" + n, [1, w], I32))
                for n, w in (("expert", blocks()), ("slot", blocks()), ("list", blocks()), ("end", NE))}
        project_phase(nc, T, gb, const, cols)
        mix_phase(nc, T, gb, const, cols, eid, rank, wts, base)
        routing_phase(nc, T, cols, eid, rank, base, dest, tabs)
        experts_phase(nc, T, const, tabs)
        combine_phase(nc, T, dest, wts)




def matrices():
    import numpy as np
    i, j = np.arange(P)[:, None], np.arange(P)[None, :]
    same = i // SL == j // SL
    m = [i == j, i <= j, i > j, (i <= j) & same, (i > j) & same, i < j, i + j >= 0]
    m = [a.astype(np.float32) for a in m]
    for s in LEVELS:
        m.append(-((i // (2 * s) == j // (2 * s)) & (i // s < j // s)).astype(np.float32))
    return np.ascontiguousarray(np.stack(m, 1))


def kernel(**inputs):
    import numpy as np
    import concourse.bacc as bacc
    from concourse.bass_utils import run_bass_kernel_spmd

    a = {k: np.asarray(v) for k, v in inputs.items()}
    NT = tiles()

    def chunks(v):
        v = v.reshape(-1, P, *v.shape[1:])
        return np.swapaxes(v, 0, 1)

    def per_row(v):
        return np.broadcast_to(v.reshape(1, -1), (P, v.size))

    conv_w = np.concatenate([a["lru_conv_w"][0], a["gdn_conv_w"][0]], 1).T
    cols = {"ln1": chunks(a["ln1_g"][0]), "ln2": chunks(a["ln2_g"][0]), "cw": chunks(conv_w).reshape(P, -1),
            "cb": chunks(a["lru_conv_b"][0]), "ba": chunks(a["lru_ba"][0]), "bx": chunks(a["lru_bx"][0]),
            "lam": chunks(a["lru_lambda"][0]), "alog": per_row(a["gdn_a_log"][0]), "dtb": per_row(a["gdn_dt_bias"][0]),
            "ng": a["gdn_norm_g"][0][:, None],
            "rb": per_row(np.concatenate([a["router_group_b"][0], a["router_expert_b"][0]])),
            "iota": per_row(np.arange(NE, dtype=np.float32)),
            "stream": (np.arange(P)[:, None] // SL == np.arange(SB)).astype(np.float32)}
    conv_s = np.concatenate([a["state_lru_conv"][0], a["state_gdn_conv"][0]], 2)
    w13 = np.concatenate([a["moe_w1"][0], a["moe_w3"][0]], 2).reshape(NE, KD, P, 2 * FE).transpose(0, 2, 1, 3)
    w2 = a["moe_w2"][0].reshape(NE, FE // P, P, D).transpose(0, 2, 1, 3)
    arrays = {
        "x": np.concatenate([a["x_prompt"].reshape(-1, D), a["x_sample"].reshape(-1, D)]),
        "mats": matrices(),
        "cols": np.concatenate([cols[k] for k in COLS], 1),
        "conv_s": conv_s.transpose(2, 0, 1).reshape(CC, P, SB, 3).transpose(1, 0, 2, 3),
        "h_s": chunks(a["state_lru_h"][0].T),
        "S_s": a["state_gdn_S"][0].transpose(2, 0, 1, 3),
        "w_in": chunks(a["w_in"][0]),
        "gates": np.concatenate([a["lru_wa"], a["lru_wx"]]),
        "w_out": chunks(a["w_out"][0]),
        "router": chunks(np.concatenate([a["router_group_w"][0], a["router_expert_w"][0]], 1)),
        "ln2_row": a["ln2_g"].reshape(1, D), "final_row": a["final_g"].reshape(1, D),
        "w13": w13.reshape(NE, P, W13), "w2": w2.reshape(NE, P, W2),
        "tokens": np.arange(NT * P, dtype=np.int32).reshape(NT, P).T,
        "block_iota": np.arange(blocks(), dtype=np.float32).reshape(1, -1),
    }
    outs = {"out_y": (NT * P, D), "out_conv_p": (P, CC, 3), "out_h_p": (P, LC), "out_S_p": (P, HEADS, P),
            "out_conv_s": (P, CC, SB, 3), "out_h_s": (P, LC, SB), "out_S_s": (P, SB, HEADS, P)}
    scratch = {"mixin": ((P, FC, NT * P), FP32), "x2": ((NT * P, D), FP32), "h2": ((NT * P, D), FP32),
               "table": ((NE * NT * P + P, 1), I32), "y": ((blocks() * P, D), FP32)}
    nc = bacc.Bacc("TRN2", target_bir_lowering=False, num_devices=1)
    T, feeds = {}, {}
    for name, v in arrays.items():
        v = np.ascontiguousarray(v)
        feeds["in_" + name] = v
        T[name] = nc.dram_tensor("in_" + name, list(v.shape), mybir.dt.from_np(v.dtype), kind="ExternalInput").ap()
    for name, shape in outs.items():
        T[name] = nc.dram_tensor(name, list(shape), FP32, kind="ExternalOutput").ap()
    for name, (shape, dt) in scratch.items():
        T[name] = nc.dram_tensor(name, list(shape), dt).ap()
    build(nc, T)
    r = run_bass_kernel_spmd(nc, [feeds], core_ids=[0]).results[0]

    def conv(v, b):
        v = np.asarray(v).reshape(P, CC, b, 3).transpose(2, 3, 1, 0)
        return (np.ascontiguousarray(v[:, :, :LC].reshape(1, b, 3, LC * P)),
                np.ascontiguousarray(v[:, :, LC:].reshape(1, b, 3, QC * P)))

    def hidden(v, b):
        return np.ascontiguousarray(np.asarray(v).reshape(P, LC, b).transpose(2, 1, 0).reshape(1, b, LC * P))

    y = np.asarray(r["out_y"])
    lp, gp = conv(r["out_conv_p"], 1)
    ls, gs = conv(r["out_conv_s"], SB)
    Sp = np.ascontiguousarray(np.asarray(r["out_S_p"]).transpose(1, 0, 2)[None, None])
    Ss = np.ascontiguousarray(np.asarray(r["out_S_s"]).transpose(1, 2, 0, 3)[None])
    return (np.ascontiguousarray(y[:SEQ].reshape(1, SEQ, D)), np.ascontiguousarray(y[SEQ:].reshape(SB, SL, D)),
            lp, hidden(r["out_h_p"], 1), gp, Sp, ls, hidden(r["out_h_s"], SB), gs, Ss)
```

```python
import concourse.bass as bass
from concourse import mybir
from contextlib import ExitStack

FP32 = mybir.dt.float32
I32 = mybir.dt.int32
U32 = mybir.dt.uint32
FP16 = mybir.dt.float16
ALU = mybir.AluOpType
ACT = mybir.ActivationFunctionType
AX = mybir.AxisListType

P = 128
D = 1024
KD = D // P
SEQ = 4096
SB, SL = 8, 16
GT = 4
GN = GT * P
HEADS = 4
LC = 4
QC = 12
CC = LC + QC
ZC = 4
FC = QC + ZC + LC
IN = 3080
NE, NGR, EPG = 32, 4, 8
FE = 256
EPS = 1e-6
LEVELS = [1, 2, 4, 8, 16, 32, 64]
W_SCALE, H_SCALE = 512.0, 16.0
PROJ = 1.0 / (W_SCALE * H_SCALE)
W13, W2 = KD * 2 * FE, (FE // P) * D

COLS = {}
_n = 0
for _name, _w in (("ln1", KD), ("ln2", KD), ("cw", CC * 4), ("cb", LC), ("ba", LC), ("bx", LC), ("lam", LC),
                  ("alog", HEADS), ("dtb", HEADS), ("ng", 1), ("rb", NGR + NE), ("iota", NE),
                  ("stream", SB)):
    COLS[_name] = (_n, _n + _w)
    _n += _w
NCOL = _n
MATS = ["ident", "upto", "after", "upto_s", "after_s", "before", "ones"] + [f"level{s}" for s in LEVELS]
NMAT = len(MATS)


def tiles():
    return SEQ // P + 1


def blocks():
    n = -(-(2 * tiles() * P + NE * (P - 1)) // P)
    return n + n % 2


class Steps:

    def __init__(self, sem, names, lead=1):
        self.sem, self.names, self.next, self.lead = sem, names, 0, lead

    def did(self, name):
        assert self.names[self.next] == name, (name, self.names[self.next])
        self.next = (self.next + 1) % len(self.names)
        return self.sem, 1

    def at(self, name, turn, back=0):
        n = len(self.names)
        return self.sem, turn * n + ((self.lead - back) * n + self.names.index(name) + 1)

    def begin(self, engine):
        engine.sem_inc(self.sem, self.lead * len(self.names))


def sequence():
    out = [("Y", 0), ("X", 0), ("Y", 1), ("X", 1), ("G", 0), ("Y", 2), ("X", 2), ("R", 0), ("G", 1), ("Y", 3), ("X", 3),
           ("O", 0), ("R", 1), ("G", 2), ("Q", 0), ("O", 1), ("R", 2), ("G", 3), ("Q", 1), ("S", 0), ("O", 2), ("R", 3),
           ("Q", 2), ("S", 1), ("O", 3)]
    for m in range(3, QC):
        out += [("Q", m), ("S", m - 1)] + [("N", 0)] * (m == 6) + [("B", 0)] * (m == 9)
    return out + [("Z", 0), ("S", QC - 1), ("Z", 1), ("Z", 2), ("Z", 3)]


def project_phase(nc, T, gb, const, cols):
    seq = sequence()
    chunks = [s for s in seq if s[0] in "YXQZ"]
    number = {s: n for n, s in enumerate(chunks)}
    NPB = 3
    column = {"X": 0, "Y": LC * P, "Q": 2 * LC * P, "Z": 2 * LC * P + QC * P}
    groups = SEQ // GN
    with ExitStack() as ctx:
        def sb(name, shape, dt=FP32):
            return ctx.enter_context(nc.sbuf_tensor(name, shape, dt))

        def sem(name):
            return ctx.enter_context(nc.semaphore(name))

        w_hi = sb("w_hi", [P, KD, IN], FP16)
        w_lo = sb("w_lo", [P, KD, IN], FP16)
        stage = sb("stage", [P, 2, KD, P])
        xt = sb("xt", [P, GT, D])
        h_hi = sb("h_hi", [P, KD, GN], FP16)
        h_lo = sb("h_lo", [P, KD, GN], FP16)
        ln16 = sb("ln16", [P, KD])
        junk = sb("junk", [P, D])
        win = sb("win", [P, 4, GN + 3])
        cv = sb("cv", [P, 4, GN])
        qo = sb("qo", [P, 4, GN])
        gy = sb("gy", [P, LC, GN])
        rg = sb("rg", [P, GN])
        ig = sb("ig", [P, 2, GN])
        la = sb("la", [P, 2, GN])
        th = sb("th", [P, 2, GN])
        oa = sb("oa", [P, 2, GN])
        asq = sb("asq", [P, GN])
        gates = sb("gates", [P, 2, LC, P])
        ss = sb("ss", [P, GT])
        rs = sb("rs", [P, GT])
        neghalf = sb("neghalf", [P, GT])
        eps = sb("eps", [P, GT])
        carry = sb("carry", [P, CC, 3])
        carry_s = sb("carry_s", [P, CC, SB, 3])
        hl = sb("hl", [P, LC])
        hl_s = sb("hl_s", [P, LC, SB])
        sp8 = sb("sp8", [P, LC])
        nsp8 = sb("nsp8", [P, LC])
        nea = sb("nea", [P, HEADS])
        asum = sb("asum", [P, GT, HEADS])
        aabs = sb("aabs", [P, GT, HEADS])
        aexp = sb("aexp", [P, GT, HEADS])
        alog1 = sb("alog1", [P, GT, HEADS])
        amax = sb("amax", [P, GT, HEADS])
        pT = [ctx.enter_context(nc.psum_tensor(f"pT{n}", [P, GN], FP32)) for n in range(2)]
        pP = [ctx.enter_context(nc.psum_tensor(f"pP{n}", [P, GN], FP32)) for n in range(NPB)]
        pG = [ctx.enter_context(nc.psum_tensor(f"pG{n}", [P, GN], FP32)) for n in range(2)]
        turned = pT + pG
        pB = ctx.enter_context(nc.psum_tensor("pB", [P, GT, 2 * HEADS], FP32))

        ident = const[:, MATS.index("ident"), :]

        def col(name, n=0, w=1):
            return cols[:, COLS[name][0] + n:COLS[name][0] + n + w]

        pe_names = [f"T{k}" for k in range(KD)] + [f"{a}{b}" for a, b in seq if a in "YXQZGB"]
        act_names = [f"T{k}" for k in range(KD)] + [f"{a}{b}" for a, b in seq if a in "YXQZGRSB"]
        dve_names = [f"L{k}" for k in range(KD)] + [n for a, b in seq if a in "XGRQB"
                                                   for n in (("Ba", "B") if a == "B" else (f"{a}{b}",))]
        pe_did = Steps(sem("project_pe"), pe_names)
        act_did = Steps(sem("project_act"), act_names)
        dve_did = Steps(sem("project_dve"), dve_names)
        ss_did = Steps(sem("norm_act"), ["ss"])
        rs_did = Steps(sem("norm_pool"), ["rs"])
        xs_did = Steps(sem("norm_dve"), ["xs"])
        wblocks = [(column[a] + m * P, P) for a, m in chunks]
        wblocks.insert(number["Q", 9] + 1, (IN - 2 * HEADS, 2 * HEADS))
        block_of = {c: wblocks.index((column[c[0]] + c[1] * P, P)) for c in chunks}
        block_of["B", 0] = number["Q", 9] + 1
        w_split = sem("w_split")
        w_hi_ready = sem("w_hi_ready")
        weights_in = [sem(f"weights_in{n}") for n in range(2)]
        setup_in = sem("setup_in")
        gates_in = sem("gates_in")
        zeroed = sem("zeroed")
        gates_zero = sem("gates_zero")
        params = sem("params")
        x_in = [sem(f"x_in{t}") for t in range(GT)]
        qo_out = [sem(f"qo_out{n}") for n in range(4)]
        oa_out = [sem(f"oa_out{n}") for n in range(2)]
        states_out = sem("states_out")
        carries_ready = sem("carries_ready")
        table_out = sem("table_out")

        block = ctx.enter_context(nc.Block())

        @block.sync
        def _(sp):
            def load(g, n):
                for t in range(n):
                    sp.wait_ge(*pe_did.at(f"T{KD - 1}", g, back=1))
                    sp.dma_start(xt[:, t, :], T["x"][bass.ts(g * GT + t, P), :]).then_inc(x_in[t], 16)

            load(0, GT)
            sp.dma_start(const[:, :, :], T["mats"]).then_inc(setup_in, 16)
            sp.dma_start(cols[:, :], T["cols"]).then_inc(setup_in, 16)
            sp.dma_start(carry_s[:, :, :, :], T["conv_s"]).then_inc(setup_in, 16)
            sp.dma_start(hl_s[:, :, :], T["h_s"]).then_inc(setup_in, 16)
            for n, (c, w) in enumerate(wblocks):
                if n == 2:
                    sp.wait_ge(gates_zero, 1)
                    for g in range(2):
                        for b in range(2):
                            for m in range(LC):
                                sp.dma_start(gates[64 * b:64 * b + 64, g, m, 64 * b:64 * b + 64],
                                             T["gates"][g, 2 * m + b]).then_inc(gates_in, 16)
                if n == 6:
                    load(1, GT)
                if n >= 2:
                    sp.wait_ge(w_split, n - 1)
                sp.dma_start(stage[:, n % 2, :, 0:w], T["w_in"][:, :, c:c + w]).then_inc(weights_in[n % 2], 16)
            with sp.Fori(2, groups) as g:
                load(g, GT)
            load(groups, 1)
            sp.wait_ge(zeroed, 1)
            n = T["table"].shape[0] // P
            done = 0
            while done < n:
                w = min(n - done, GN)
                sp.dma_start(T["table"][done * P:(done + w) * P, 0].rearrange("(p n) -> p n", p=P),
                             junk[:, 0:w].bitcast(I32)).then_inc(table_out, 16)
                done += w
            sp.wait_ge(table_out, 16 * -(-n // GN))
            sp.wait_ge(carries_ready, 1)
            for dst, src in (("out_conv_p", carry[:, :, :]), ("out_h_p", hl[:, :]),
                             ("out_conv_s", carry_s[:, :, :, :]), ("out_h_s", hl_s[:, :, :])):
                sp.dma_start(T[dst], src).then_inc(states_out, 16)
            sp.wait_ge(states_out, 64)

        @block.gpsimd
        def _(pool):
            rs_did.begin(pool)
            nc.gpsimd.memset(gates[:, :, :, :], 0.0).then_inc(gates_zero, 1)
            nc.gpsimd.memset(neghalf[:, :], -0.5)
            nc.gpsimd.memset(eps[:, :], EPS)
            pool.drain()

            def group(g, n):
                pool.wait_ge(*ss_did.at("ss", g))
                nc.gpsimd.tensor_tensor(ss[:, 0:n], ss[:, 0:n], eps[:, 0:n], ALU.add)
                pool.drain()
                pool.wait_ge(*xs_did.at("xs", g, back=1))
                nc.gpsimd.tensor_tensor(rs[:, 0:n], ss[:, 0:n], neghalf[:, 0:n], ALU.pow).then_inc(*rs_did.did("rs"))

            with pool.Fori(0, groups) as g:
                group(g, GT)
            group(groups, 1)

        @block.tensor
        def _(pe):
            pe_did.begin(pe)
            PARTS = ((w_hi, h_hi), (w_hi, h_lo), (w_lo, h_hi))
            pe.wait_ge(setup_in, 16 * 4)

            def group(g, nt, first=False):
                N = nt * P
                pe.wait_ge(*xs_did.at("xs", g))
                for k in range(KD):
                    if k >= 4:
                        pe.wait_ge(*dve_did.at(f"L{k - 4}", g))
                    elif k >= 2:
                        pe.wait_ge(*act_did.at(f"G{LC - 1}", g, back=1))
                    else:
                        pe.wait_ge(*dve_did.at(f"L{k + 4}", g, back=1))
                    for t in range(nt):
                        ins = nc.tensor.transpose(turned[k % 4][:, t * P:(t + 1) * P], xt[:, t, k * P:(k + 1) * P], ident)
                    ins.then_inc(*pe_did.did(f"T{k}"))
                pe.wait_ge(*dve_did.at(f"L{KD - 1}", g))
                for kind, m in seq:
                    if kind in "YXQZ":
                        n = number[kind, m]
                        before = chunks[n - NPB]
                        pe.wait_ge(*act_did.at(f"{before[0]}{before[1]}", g, back=int(n < NPB)))
                        if first:
                            pe.wait_ge(w_split, block_of[kind, m] + 1)
                        c0 = column[kind] + m * P
                        for k in range(KD):
                            for i, (w, h) in enumerate(PARTS):
                                ins = nc.tensor.matmul(pP[n % NPB][:, 0:N], w[:, k, c0:c0 + P], h[:, k, 0:N],
                                                       start=(k + i == 0), stop=(k == KD - 1 and i == 2))
                        ins.then_inc(*pe_did.did(f"{kind}{m}"))
                    elif kind == "G":
                        if first and m == 0:
                            pe.wait_ge(gates_in, 16 * 4 * LC)
                        pe.wait_ge(*dve_did.at(f"X{m}", g))
                        pe.wait_ge(*act_did.at(f"G{(m - 1) % LC}", g, back=int(m == 0)))
                        for b in range(2):
                            ins = nc.tensor.matmul(pG[b][:, 0:N], gates[:, b, m, :], cv[:, m, 0:N], start=True, stop=True)
                        ins.then_inc(*pe_did.did(f"G{m}"))
                    elif kind == "B":
                        if first:
                            pe.wait_ge(w_split, block_of["B", 0] + 1)
                        pe.wait_ge(*dve_did.at("B", g, back=1))
                        pe.wait_ge(*act_did.at("B0", g, back=1))
                        for t in range(nt):
                            for k in range(KD):
                                for i, (w, h) in enumerate(PARTS):
                                    ins = nc.tensor.matmul(pB[:, t, :], h[:, k, t * P:(t + 1) * P],
                                                           w[:, k, IN - 2 * HEADS:IN],
                                                           start=(k + i == 0), stop=(k == KD - 1 and i == 2))
                        ins.then_inc(*pe_did.did("B0"))

            group(0, GT, first=True)
            with pe.Fori(1, groups) as g:
                group(g, GT)
            group(groups, 1)

        def shaped(ap, stream):
            return ap.rearrange("p (s l) -> p s l", s=SB) if stream else ap

        def window(m, off, stream):
            if stream:
                return win[:, m % 4, 0:SB * (SL + 3)].rearrange("p (s l) -> p s l", s=SB)[:, :, off:off + SL]
            return win[:, m % 4, off:off + GN]

        @block.scalar
        def _(act):
            act_did.begin(act)
            ss_did.begin(act)
            def norm(g, nt):
                for t in range(nt):
                    act.drain()
                    act.wait_ge(x_in[t], (g + 1) * 16)
                    if t == 0:
                        act.wait_ge(*rs_did.at("rs", g, back=1))
                    ins = nc.scalar.activation(junk[:, :], xt[:, t, :], ACT.Square, scale=D ** -0.5,
                                               accum_out=ss[:, t:t + 1])
                ins.then_inc(*ss_did.did("ss"))

            def split(n):
                c, w = wblocks[n]
                act.wait_ge(weights_in[n % 2], 16 * (n // 2 + 1))
                nc.scalar.activation(w_hi[:, :, c:c + w], stage[:, n % 2, :, 0:w], ACT.Copy, scale=W_SCALE
                                     ).then_inc(w_hi_ready, 1)

            def group(g, nt, stream, following, first=False):
                N = nt * P
                for k in range(KD):
                    act.wait_ge(*pe_did.at(f"T{k}", g))
                    nc.scalar.activation(h_hi[:, k, 0:N], turned[k % 4][:, 0:N], ACT.Copy, scale=ln16[:, k:k + 1]
                                         ).then_inc(*act_did.did(f"T{k}"))

                def store(chunk, src, done):
                    act.dma_start(T["mixin"][:, chunk, bass.ds(g * GN, N)], src).then_inc(done, 16)

                for kind, m in seq:
                    if first and block_of.get((kind, m), len(wblocks)) + 2 < len(wblocks):
                        split(block_of[kind, m] + 2)
                    if kind == "N" and following:
                        norm(g + 1, following)
                    elif kind == "Y":
                        act.wait_ge(*pe_did.at(f"Y{m}", g))
                        act.wait_ge(*dve_did.at(f"R{m}", g, back=1))
                        nc.scalar.activation(gy[:, m, 0:N], pP[number[kind, m] % NPB][:, 0:N], ACT.Gelu_apprx_tanh,
                                             scale=PROJ).then_inc(*act_did.did(f"Y{m}"))
                    elif kind in "XQ":
                        c = m if kind == "X" else LC + m
                        o = (c - 4) % CC
                        act.wait_ge(*pe_did.at(f"{kind}{m}", g))
                        act.wait_ge(*dve_did.at(f"X{o}" if o < LC else f"Q{o - LC}", g, back=int(c < 4)))
                        nc.scalar.activation(window(c, 3, stream), shaped(pP[number[kind, m] % NPB][:, 0:N], stream),
                                             ACT.Copy, scale=PROJ).then_inc(*act_did.did(f"{kind}{m}"))
                    elif kind == "G":
                        act.drain()
                        act.wait_ge(*pe_did.at(f"G{m}", g))
                        act.wait_ge(*dve_did.at(f"R{(m - 2) % LC}", g, back=int(m < 2)))
                        nc.scalar.activation(rg[:, 0:N], pG[0][:, 0:N], ACT.Sigmoid, bias=col("ba", m))
                        nc.scalar.activation(ig[:, m % 2, 0:N], pG[1][:, 0:N], ACT.Sigmoid, bias=col("bx", m))
                        act.drain()
                        nc.scalar.activation(la[:, m % 2, 0:N], rg[:, 0:N], ACT.Exp, scale=nsp8[:, m:m + 1])
                        nc.scalar.activation(th[:, m % 2, 0:N], rg[:, 0:N], ACT.Tanh, scale=sp8[:, m:m + 1]
                                             ).then_inc(*act_did.did(f"G{m}"))
                    elif kind == "R":
                        act.wait_ge(*dve_did.at(f"G{m}", g))
                        nc.scalar.activation(th[:, m % 2, 0:N], th[:, m % 2, 0:N], ACT.Sqrt
                                             ).then_inc(*act_did.did(f"R{m}"))
                    elif kind == "O":
                        act.wait_ge(*dve_did.at(f"R{m}", g))
                        store(QC + ZC + m, oa[:, m % 2, 0:N], oa_out[m % 2])
                    elif kind == "S":
                        slot = m % 4
                        act.wait_ge(*dve_did.at(f"Q{m}", g))
                        act.wait_ge(qo_out[slot], g * 64 + (m // 4 + 1) * 16)
                        nc.scalar.activation(qo[:, slot, 0:N], cv[:, slot, 0:N], ACT.Silu).then_inc(*act_did.did(f"S{m}"))
                        act.drain()
                        store(m, qo[:, slot, 0:N], qo_out[slot])
                    elif kind == "Z":
                        act.wait_ge(*pe_did.at(f"Z{m}", g))
                        act.wait_ge(qo_out[m], g * 64 + 64)
                        nc.scalar.activation(qo[:, m, 0:N], pP[number[kind, m] % NPB][:, 0:N], ACT.Silu,
                                             scale=PROJ).then_inc(*act_did.did(f"Z{m}"))
                        act.drain()
                        store(QC + m, qo[:, m, 0:N], qo_out[m])
                    elif kind == "B":
                        act.wait_ge(*pe_did.at("B0", g))
                        act.wait_ge(*dve_did.at("Ba", g))
                        nc.scalar.activation(gb[:, bass.ds(g * GT, nt), 0:HEADS], pB[:, 0:nt, 0:HEADS], ACT.Sigmoid, scale=PROJ)
                        nc.scalar.activation(aabs[:, 0:nt], asum[:, 0:nt], ACT.Abs)
                        act.drain()
                        nc.scalar.activation(aexp[:, 0:nt], aabs[:, 0:nt], ACT.Exp, scale=-1.0)
                        act.drain()
                        nc.scalar.activation(alog1[:, 0:nt], aexp[:, 0:nt], ACT.Ln, bias=1.0).then_inc(*act_did.did("B0"))

            for s in qo_out:
                act.sem_inc(s, 16)
            norm(0, GT)
            act.wait_ge(setup_in, 16 * 4)
            nc.scalar.activation(sp8[:, :], col("lam", 0, LC), ACT.Exp, scale=-1.0)
            act.drain()
            nc.scalar.activation(sp8[:, :], sp8[:, :], ACT.Ln, bias=1.0)
            nc.scalar.activation(nea[:, :], col("alog", 0, HEADS), ACT.Exp)
            act.drain()
            nc.scalar.activation(nsp8[:, :], sp8[:, :], ACT.Copy, scale=-8.0)
            nc.scalar.activation(nea[:, :], nea[:, :], ACT.Copy, scale=-1.0)
            act.drain()
            nc.scalar.activation(sp8[:, :], sp8[:, :], ACT.Copy, scale=8.0)
            nc.scalar.activation(ln16[:, :], col("ln1", 0, KD), ACT.Copy, scale=H_SCALE)
            act.drain()
            nc.scalar.copy(carry[:, 0, 0:1], sp8[:, 0:1]).then_inc(params, 1)
            split(0)
            split(1)
            group(0, GT, False, GT, first=True)
            with act.Fori(1, groups - 1) as g:
                group(g, GT, False, GT)
            group(groups - 1, GT, False, 1)
            group(groups, 1, True, 0)
            for s in qo_out:
                act.wait_ge(s, 16 + 64 * (groups + 1))
            for s in oa_out:
                act.wait_ge(s, 16 + 32 * (groups + 1))

        @block.vector
        def _(dve):
            dve_did.begin(dve)
            xs_did.begin(dve)
            for s in oa_out:
                dve.sem_inc(s, 16)
            def norm(g, nt):
                dve.wait_ge(*rs_did.at("rs", g))
                for t in range(nt):
                    ins = nc.vector.tensor_scalar(xt[:, t, :], xt[:, t, :], rs[:, t:t + 1], None, ALU.mult)
                ins.then_inc(*xs_did.did("xs"))

            def split(n):
                c, w = wblocks[n]
                dve.wait_ge(w_hi_ready, n + 1)
                nc.vector.scalar_tensor_tensor(w_lo[:, :, c:c + w], stage[:, n % 2, :, 0:w], W_SCALE,
                                               w_hi[:, :, c:c + w], ALU.mult, ALU.subtract).then_inc(w_split, 1)

            def group(g, nt, stream, following, first=False):
                N = nt * P
                for k in range(KD):
                    dve.wait_ge(*act_did.at(f"T{k}", g))
                    nc.vector.scalar_tensor_tensor(h_lo[:, k, 0:N], turned[k % 4][:, 0:N], ln16[:, k:k + 1],
                                                   h_hi[:, k, 0:N], ALU.mult, ALU.subtract).then_inc(*dve_did.did(f"L{k}"))
                kept = carry_s if stream else carry
                for kind, m in seq:
                    if first and block_of.get((kind, m), len(wblocks)) + 2 < len(wblocks):
                        split(block_of[kind, m] + 2)
                    if kind == "N" and following:
                        norm(g + 1, following)
                    elif kind in "XQ":
                        c = m if kind == "X" else LC + m
                        slot = c % 4
                        cw = lambda j: col("cw", 4 * c + j)
                        old = shaped(win[:, slot, 0:SB * (SL + 3)], True)[:, :, 0:3] if stream else win[:, slot, 0:3]
                        new = shaped(win[:, slot, 0:SB * (SL + 3)], True)[:, :, SL:SL + 3] if stream else win[:, slot, N:N + 3]
                        dst = shaped(cv[:, slot, 0:N], stream)
                        dve.wait_ge(*act_did.at(f"{kind}{m}", g))
                        if c >= 8:
                            dve.wait_ge(*act_did.at(f"S{c - 8}", g))
                        elif c < 4:
                            dve.wait_ge(*act_did.at(f"S{QC - 4 + c}", g, back=1))
                        else:
                            dve.wait_ge(*pe_did.at(f"G{m}", g))
                        nc.vector.tensor_copy(old, kept[:, c])
                        dve.drain()
                        if kind == "X":
                            nc.vector.tensor_scalar(dst, window(c, 0, stream), cw(0), col("cb", m), ALU.mult, ALU.add)
                        else:
                            nc.vector.tensor_scalar(dst, window(c, 0, stream), cw(0), None, ALU.mult)
                        nc.vector.tensor_copy(kept[:, c], new)
                        for j in range(1, 4):
                            dve.drain()
                            ins = nc.vector.scalar_tensor_tensor(dst, window(c, j, stream), cw(j), dst, ALU.mult, ALU.add)
                        ins.then_inc(*dve_did.did(f"{kind}{m}"))
                    elif kind == "G":
                        s = m % 2
                        dve.wait_ge(*act_did.at(f"G{m}", g))
                        nc.vector.tensor_tensor(asq[:, 0:N], la[:, s, 0:N], la[:, s, 0:N], ALU.mult)
                        nc.vector.tensor_tensor(ig[:, s, 0:N], ig[:, s, 0:N], cv[:, m, 0:N], ALU.mult)
                        dve.drain()
                        nc.vector.scalar_tensor_tensor(th[:, s, 0:N], asq[:, 0:N], 1.0, th[:, s, 0:N], ALU.add, ALU.mult
                                                       ).then_inc(*dve_did.did(f"G{m}"))
                    elif kind == "R":
                        s = m % 2
                        dve.wait_ge(*act_did.at(f"R{m}", g))
                        dve.wait_ge(oa_out[s], g * 32 + (m // 2 + 1) * 16)
                        nc.vector.tensor_tensor(ig[:, s, 0:N], ig[:, s, 0:N], th[:, s, 0:N], ALU.mult)
                        dve.drain()
                        if stream:
                            for b in range(SB):
                                r = slice(b * SL, (b + 1) * SL)
                                nc.vector.tensor_tensor_scan(oa[:, s, r], la[:, s, r], ig[:, s, r], hl_s[:, m, b:b + 1],
                                                             ALU.mult, ALU.add)
                            dve.drain()
                            nc.vector.tensor_copy(hl_s[:, m, :], shaped(oa[:, s, 0:N], True)[:, :, SL - 1])
                        else:
                            nc.vector.tensor_tensor_scan(oa[:, s, 0:N], la[:, s, 0:N], ig[:, s, 0:N], hl[:, m:m + 1],
                                                         ALU.mult, ALU.add)
                            dve.drain()
                            nc.vector.tensor_copy(hl[:, m:m + 1], oa[:, s, N - 1:N])
                        dve.drain()
                        dve.wait_ge(*act_did.at(f"Y{m}", g))
                        nc.vector.tensor_tensor(oa[:, s, 0:N], oa[:, s, 0:N], gy[:, m, 0:N], ALU.mult
                                                ).then_inc(*dve_did.did(f"R{m}"))
                    elif kind == "B":
                        dve.wait_ge(*pe_did.at("B0", g))
                        dtb = col("dtb", 0, HEADS).unsqueeze(1).to_broadcast([P, nt, HEADS])
                        neg = nea[:, :].unsqueeze(1).to_broadcast([P, nt, HEADS])
                        nc.vector.scalar_tensor_tensor(asum[:, 0:nt], pB[:, 0:nt, HEADS:], PROJ, dtb, ALU.mult, ALU.add
                                                       ).then_inc(*dve_did.did("Ba"))
                        dve.drain()
                        dve.wait_ge(*act_did.at("B0", g))
                        nc.vector.scalar_tensor_tensor(amax[:, 0:nt], asum[:, 0:nt], 0.0, alog1[:, 0:nt], ALU.max, ALU.add)
                        dve.drain()
                        nc.vector.tensor_tensor(gb[:, bass.ds(g * GT, nt), HEADS:], amax[:, 0:nt], neg, ALU.mult
                                                ).then_inc(*dve_did.did("B"))

            norm(0, GT)
            dve.wait_ge(params, 1)
            nc.vector.memset(carry[:, :, :], 0.0)
            nc.vector.memset(hl[:, :], 0.0)
            dve.drain()
            split(0)
            split(1)
            group(0, GT, False, GT, first=True)
            with dve.Fori(1, groups - 1) as g:
                group(g, GT, False, GT)
            group(groups - 1, GT, False, 1)
            group(groups, 1, True, 0)
            dve.drain()
            nc.vector.tensor_copy(rs[:, 0:1], hl[:, 0:1]).then_inc(carries_ready, 1)
            dve.wait_ge(*ss_did.at("ss", groups))
            nc.vector.memset(junk[:, :], 0.0).then_inc(zeroed, 1)


MIX = """
X.sq.act X.gs.dve
Y.KS.pe Y.QS.pe Y.X.dve R.x2.dve Y.o1.act R.st.act R.r2.pool
X.stat.pe X.dec.pe X.sse.dve X.ex.act X.DT.act X.rr.pool R.xn.dve R.h2.pool
Y.N.pe Y.vd.dve Y.vh.act
X.kt.pe X.ktc.act X.vt.pe X.sc.dve
R.hT0.pe R.hT1.pe R.hc0.dve R.hc1.dve
Y.dS.pe Y.S.dve Y.AV.pe
X.KK.pe X.QK.pe X.vs.act X.G.dve X.B2.pool X.Z1.dve Y.o.dve X.AT.dve
R.lg.pe Y.so.act Y.ro.pool R.r0.dve R.sh.act
Y.outA2.pe X.B4.pool
X.T1.pe X.T1c.act R.r1.dve R.rx.act Y.on.dve
Y.outA3.pe X.ATm.pool
X.W2.pe X.I2.dve Y.outA0.pe
X.T2.pe X.T2c.act Y.outA1.pe Y.oT.pe X.B8.pool
X.W4.pe X.Z2.pe X.Z2c.act Y.mx.dve X.I4.dve Y.outB0.pe X.B16.pool
X.T4.pe X.T4c.act Y.outB1.pe X.B32.pool
X.W8.pe X.Z4.pe X.Z4c.act X.I8.dve R.r3.dve Y.outB2.pe
X.T8.pe X.T8c.act Y.outB3.pe X.B64.pool
X.W16.pe X.Z8.pe X.Z8c.act X.I16.dve R.rk.pe
X.T16.pe X.T16c.act Y.outB4.pe R.off.dve
X.W32.pe X.Z16.pe X.Z16c.act X.I32.dve Y.outB5.pe R.sct.pool
X.T32.pe X.T32c.act Y.outB6.pe
X.W64.pe X.Z32.pe X.Z32c.act X.I64.dve Y.outB7.pe
X.Z64.pe X.Z64c.act
""".split()
MIX = [tuple(s.split(".")) for s in MIX]
ENGINES = ("pe", "act", "dve", "pool")


def mix_phase(nc, T, gb, const, cols, eid, rank, wts, base):
    NT = tiles()
    H = HEADS
    with ExitStack() as ctx:
        def sb(name, shape, dt=FP32):
            return ctx.enter_context(nc.sbuf_tensor(name, shape, dt))

        def sem(name):
            return ctx.enter_context(nc.semaphore(name))

        w_out = sb("w_out", [P, KD, D])
        router = sb("router", [P, KD, P])
        ln2_row = sb("ln2_row", [P, D])
        tok = sb("tok", [P, NT], I32)
        ft = [sb(f"ft{p}", [P, FC, P]) for p in range(2)]
        xr = [sb(f"xr{p}", [P, D]) for p in range(2)]
        sqb = sb("sqb", [P, 2 * H, P])
        gt = [sb(f"gt{p}", [P, 2 * H]) for p in range(2)]
        gw = sb("gw", [P, P])
        gsel = sb("gsel", [P, SB, H])
        gs = sb("gs", [P, H, P])
        DT = sb("DT", [P, H, P])
        G = sb("G", [P, H, P])
        Bs = {s: sb(f"B{s}", [P, H, P]) for s in LEVELS}
        Tm = sb("Tm", [P, H, P])
        Zm = sb("Zm", [P, H, P])
        WI = sb("WI", [P, H, P])
        Zf = [sb(f"Zf{p}", [P, H, P]) for p in range(2)]
        AT = [sb(f"AT{p}", [P, H, P]) for p in range(2)]
        ktok = [sb(f"ktok{p}", [P, H, P]) for p in range(2)]
        vs = [sb(f"vs{p}", [P, H, P]) for p in range(2)]
        sse = sb("sse", [P, 2 * H])
        rr = sb("rr", [P, 2 * H])
        ex = [sb(f"ex{p}", [P, 3 * H + SB * H]) for p in range(2)]
        sc = [sb(f"sc{p}", [P, 7, H]) for p in range(2)]
        S = sb("S", [P, H, P])
        S_s = sb("S_s", [P, SB, H, P])
        kz = sb("kz", [P, H, SB, P])
        vm = sb("vm", [P, H, P])
        xb = sb("xb", [P, H, P])
        vhat = sb("vhat", [P, H, P])
        vdec = sb("vdec", [P, H, P])
        o1 = sb("o1", [P, H, P])
        ob = sb("ob", [P, H, P])
        onb = sb("onb", [P, H, P])
        mx = sb("mx", [P, H, P])
        junk = sb("junk2", [P, D])
        so = sb("so", [P, H])
        ro = sb("ro", [P, H])
        neghalf = sb("neghalf2", [P, 2 * H])
        eps = sb("eps2", [P, 2 * H])
        x2b = sb("x2b", [P, D])
        xn = sb("xn", [P, D])
        h2b = sb("h2b", [P, D])
        s2 = sb("s2", [P, 1])
        rs2 = sb("rs2", [P, 1])
        hT = sb("hT2", [P, KD, P])
        lg = sb("lg", [P, NE])
        gpad = sb("gpad", [P, 8])
        m8 = sb("m8", [P, 8])
        i8 = sb("i8", [P, 8], U32)
        gid = sb("gid", [P, 1])
        gid8 = sb("gid8", [P, 1])
        goh = sb("goh", [P, NGR])
        esel = sb("esel", [P, EPG])
        m8e = sb("m8e", [P, 8])
        i8e = sb("i8e", [P, 8], U32)
        ief = sb("ief", [P, 2])
        e2 = sb("e2", [P, 2])
        dif = sb("dif", [P, NGR + 1])
        exd = sb("exd", [P, NGR + 1])
        sg = sb("sg", [P, 1])
        den = sb("den", [P, 1])
        w2t = sb("w2t", [P, 2])
        O0 = sb("O0", [P, NE])
        O1 = sb("O1", [P, NE])
        OO = sb("OO", [P, NE])
        rkf = sb("rkf", [P, NE])
        rjunk = sb("rjunk", [P, NE])
        r2t = sb("r2t", [P, 2])
        offs = [sb(f"offs{k}", [P, 1], I32) for k in range(2)]
        tid = sb("tid", [P, 1], I32)
        XA, XB, XC, YA, YB, YC, YD, YE = [
            ctx.enter_context(nc.psum_tensor(f"bank{n}", [P, H, P], FP32)) for n in range(8)]
        flat = lambda b: b[:, :, :].rearrange("p h n -> p (h n)")

        done = {(st, e): Steps(sem(f"mix_{st}_{e}"), [n for a, n, b in MIX if a == st and b == e], lead=2)
                for st in "XYR" for e in ENGINES if any(a == st and b == e for a, n, b in MIX)}
        owner = {n: done[st, e] for st, n, e in MIX}
        weights_in = sem("mix_weights_in")
        w_out_in = sem("w_out_in")
        S_s_in = sem("S_s_in")
        ft_in = [sem(f"ft_in{p}") for p in range(2)]
        xr_in = [sem(f"xr_in{p}") for p in range(2)]
        x2_out = sem("x2_out")
        h2_out = sem("h2_out")
        ids_out = sem("ids_out")
        scatters = sem("scatters")
        spread = sem("spread")
        vm_ready = sem("vm_ready")
        stream_S = sem("stream_S")
        stream_mm = sem("stream_mm")
        S_out = sem("S_out")
        S_ready = sem("S_ready")
        const2 = sem("const2")

        def at(name, t, back=0):
            return owner[name].at(name, t, back)

        def mat(name):
            return const[:, MATS.index(name), :]

        def heads(ap):
            return ap.unsqueeze(1).to_broadcast([P, H, P])

        def per_head(ap):
            return ap.unsqueeze(2).to_broadcast([P, H, P])

        def col(name, n=0, w=1):
            return cols[:, COLS[name][0] + n:COLS[name][0] + n + w]

        def program(engine, begin, x_step, y_step):
            for (st, e), d in done.items():
                if e == engine:
                    d.begin(begin)

            def run(x, y, r):
                for st, n, e in MIX:
                    tile = {"X": x, "Y": y, "R": r}[st]
                    if e == engine and tile is not None:
                        (x_step if st == "X" else y_step)(n, tile[0], tile[1], tile[2], done[st, e].did)

            last = NT - 1
            run((0, 0, False), None, None)
            run((1, 1, False), (0, 0, False), None)
            with begin.Fori(0, (last - 2) // 2) as pair:
                t = pair * 2
                run((t + 2, 0, False), (t + 1, 1, False), (t, 0, False))
                run((t + 3, 1, False), (t + 2, 0, False), (t + 1, 1, False))
            run((last, 0, True), (last - 1, 1, False), (last - 2, 0, False))
            run(None, (last, 0, True), (last - 1, 1, False))
            run(None, None, (last, 0, True))

        block = ctx.enter_context(nc.Block())

        @block.sync
        def _(sp):
            def load(t, p):
                sp.wait_ge(*at("outA1", t, 2))
                sp.wait_ge(*at("mx", t, 2))
                sp.dma_start(ft[p][:, :, :], T["mixin"][:, :, bass.ts(t, P)]).then_inc(ft_in[p], 16)
                sp.wait_ge(*at("x2", t, 2))
                sp.dma_start(xr[p][:, :], T["x"][bass.ts(t, P), :]).then_inc(xr_in[p], 16)

            sp.dma_start(ft[0][:, :, :], T["mixin"][:, :, 0:P]).then_inc(ft_in[0], 16)
            sp.dma_start(router[:, :, :], T["router"]).then_inc(weights_in, 16)
            sp.dma_start(ln2_row[:, :], T["ln2_row"].to_broadcast([P, D])).then_inc(weights_in, 16)
            sp.dma_start(tok[:, :], T["tokens"]).then_inc(weights_in, 16)
            sp.dma_start(xr[0][:, :], T["x"][0:P, :]).then_inc(xr_in[0], 16)
            sp.dma_start(w_out[:, :, :], T["w_out"]).then_inc(w_out_in, 16)
            sp.dma_start(S_s[:, :, :, :], T["S_s"]).then_inc(S_s_in, 16)
            with sp.Fori(0, (NT - 1) // 2) as pair:
                load(pair * 2 + 1, 1)
                load(pair * 2 + 2, 0)
            sp.wait_ge(S_ready, 1)
            sp.dma_start(T["out_S_p"], S[:, :, :]).then_inc(S_out, 16)
            sp.wait_ge(S_ready, 2)
            sp.dma_start(T["out_S_s"], S_s[:, :, :, :]).then_inc(S_out, 16)
            sp.wait_ge(S_out, 32)

        def ft_turn(t, p):
            return (t - p) * 8 + 16

        @block.tensor
        def _(pe):
            ident = mat("ident")

            def x_step(n, t, p, stream, did):
                q, k, v = (lambda h: ft[p][:, h, :]), (lambda h: ft[p][:, H + h, :]), (lambda h: ft[p][:, 2 * H + h, :])
                if n == "stat":
                    pe.wait_ge(*at("I64", t, 1))
                    pe.wait_ge(*at("sq", t))
                    for c in range(2 * H):
                        nc.tensor.matmul(flat(XB)[:, c:c + P], sqb[:, c, :], mat("ones"), start=True, stop=True)
                    pe.wait_ge(*at("gs", t))
                    g = gw[:, :]
                    c = 2 * H
                    for m in ("upto_s" if stream else "upto", "after_s" if stream else "after", "ones"):
                        ins = nc.tensor.matmul(flat(XB)[:, c:c + P], mat(m), g, start=True, stop=True)
                        c += H
                    if stream:
                        ins = nc.tensor.matmul(flat(XB)[:, c:c + SB * H], mat("ones"),
                                               gsel[:, :, :].rearrange("p s h -> p (s h)"), start=True, stop=True)
                    ins.then_inc(*did(n))
                elif n == "dec":
                    pe.wait_ge(*at("Z64c", t, 1))
                    for h in range(H):
                        ins = nc.tensor.matmul(XA[:, h, :], gs[:, h, :], mat("upto_s" if stream else "upto"),
                                               start=True, stop=True)
                    ins.then_inc(*did(n))
                elif n == "kt":
                    pe.wait_ge(*at("T32c", t, 1))
                    for h in range(H):
                        ins = nc.tensor.transpose(XC[:, h, :], k(h), ident)
                    ins.then_inc(*did(n))
                elif n == "vt":
                    pe.wait_ge(*at("ex", t))
                    for h in range(H):
                        ins = nc.tensor.transpose(XB[:, h, :], v(h), ident)
                    ins.then_inc(*did(n))
                elif n == "KK":
                    pe.wait_ge(*at("DT", t))
                    for h in range(H):
                        ins = nc.tensor.matmul(XA[:, h, :], k(h), k(h), start=True, stop=True)
                    ins.then_inc(*did(n))
                elif n == "QK":
                    pe.wait_ge(*at("ktc", t))
                    for h in range(H):
                        ins = nc.tensor.matmul(XC[:, h, :], k(h), q(h), start=True, stop=True)
                    ins.then_inc(*did(n))
                elif n == "T1":
                    pe.wait_ge(*at("Z1", t))
                    for h in range(H):
                        ins = nc.tensor.transpose(XA[:, h, :], Zm[:, h, :], ident)
                    ins.then_inc(*did(n))
                elif n[0] == "W":
                    s = int(n[1:])
                    if s == 2:
                        pe.wait_ge(*at("vs", t))
                    else:
                        pe.wait_ge(*at(f"I{s // 2}", t))
                    pe.wait_ge(*at(f"B{s}", t))
                    pe.wait_ge(*at(f"T{s // 2}c", t))
                    for h in range(H):
                        ins = nc.tensor.matmul(XB[:, h, :], Bs[s][:, h, :], Tm[:, h, :], start=True, stop=True)
                    ins.then_inc(*did(n))
                elif n[0] == "T":
                    s = int(n[1:])
                    if s == 2:
                        pe.wait_ge(*at("AT", t))
                    pe.wait_ge(*at(f"I{s}", t))
                    if s > 2:
                        pe.wait_ge(*at(f"Z{s // 2}c", t))
                    for h in range(H):
                        ins = nc.tensor.matmul(XC[:, h, :], Zm[:, h, :], WI[:, h, :], start=True, stop=True)
                    ins.then_inc(*did(n))
                elif n[0] == "Z" and n != "Z64":
                    s = int(n[1:])
                    pe.wait_ge(*at(f"T{s}c", t))
                    for h in range(H):
                        ins = nc.tensor.transpose(XA[:, h, :], Tm[:, h, :], ident)
                    ins.then_inc(*did(n))
                elif n == "Z64":
                    pe.wait_ge(*at("I64", t))
                    pe.wait_ge(*at("Z32c", t))
                    for h in range(H):
                        ins = nc.tensor.matmul(XA[:, h, :], WI[:, h, :], Zm[:, h, :], start=True, stop=True)
                    ins.then_inc(*did(n))

            def y_step(n, t, p, stream, did):
                if n in ("KS", "QS"):
                    if n == "KS":
                        pe.wait_ge(*at("off", t, 2))
                        pe.wait_ge(*at("S", t, 1))
                        pe.wait_ge(ft_in[p], ft_turn(t, p))
                    else:
                        pe.wait_ge(*at("o", t, 1))
                    bank = YA if n == "KS" else YB
                    if stream:
                        pe.wait_ge(S_s_in, 16)
                        pe.wait_ge(spread, 1 if n == "KS" else 2)
                    for h in range(H):
                        if stream:
                            for b in range(SB):
                                ins = nc.tensor.matmul(bank[:, h, :], kz[:, h, b, :], S_s[:, b, h, :],
                                                       start=(b == 0), stop=(b == SB - 1))
                        else:
                            ins = nc.tensor.matmul(bank[:, h, :], ft[p][:, (H if n == "KS" else 0) + h, :], S[:, h, :],
                                                   start=True, stop=True)
                    ins.then_inc(*did(n))
                elif n == "N":
                    pe.wait_ge(*at("Z64c", t))
                    pe.wait_ge(*at("X", t))
                    for h in range(H):
                        ins = nc.tensor.matmul(YA[:, h, :], Zf[p][:, h, :], xb[:, h, :], start=True, stop=True)
                    ins.then_inc(*did(n))
                elif n == "dS":
                    pe.wait_ge(*at("mx", t, 1))
                    pe.wait_ge(*at("vd", t))
                    if stream:
                        for b in range(SB):
                            pe.wait_ge(vm_ready, b + 1)
                            for h in range(H):
                                ins = nc.tensor.matmul(YC[:, h, :], ktok[p][:, h, :], vm[:, h, :], start=True, stop=True)
                            ins.then_inc(stream_mm, 1)
                            pe.wait_ge(stream_S, b + 1)
                    for h in range(H):
                        ins = nc.tensor.matmul(YC[:, h, :], ktok[p][:, h, :], vdec[:, h, :], start=True, stop=True)
                    ins.then_inc(*did(n))
                elif n == "AV":
                    pe.wait_ge(*at("o1", t))
                    pe.wait_ge(*at("vh", t))
                    pe.wait_ge(*at("ATm", t))
                    for h in range(H):
                        ins = nc.tensor.matmul(YB[:, h, :], AT[p][:, h, :], vhat[:, h, :], start=True, stop=True)
                    ins.then_inc(*did(n))
                elif n[:-1] == "outA":
                    half, c0 = divmod(int(n[-1]), 2)
                    if isinstance(t, int) and t == 0:
                        pe.wait_ge(w_out_in, 16)
                    pe.wait_ge(*at("x2", t, 1))
                    pe.wait_ge(*at("r0" if half == 0 else "hc1", t, 1))
                    for c in (2 * c0, 2 * c0 + 1):
                        ins = nc.tensor.matmul(flat((YD, YE)[half]), ft[p][:, QC + ZC + c, :],
                                               w_out[:, c, half * 512:half * 512 + 512], start=(c == 0), stop=False)
                    ins.then_inc(*did(n))
                elif n == "oT":
                    pe.wait_ge(*at("S", t))
                    pe.wait_ge(*at("on", t))
                    for h in range(H):
                        ins = nc.tensor.transpose(YC[:, h, :], onb[:, h, :], ident)
                    ins.then_inc(*did(n))
                elif n[:-1] == "outB":
                    pe.wait_ge(*at("mx", t))
                    half, h = divmod(int(n[-1]), H)
                    nc.tensor.matmul(flat((YD, YE)[half]), mx[:, h, :], w_out[:, LC + h, half * 512:half * 512 + 512],
                                     start=False, stop=(h == H - 1)).then_inc(*did(n))
                elif n in ("hT0", "hT1"):
                    half = int(n[-1])
                    pe.wait_ge(*at("xn", t))
                    for c in range(4):
                        k = 4 * half + c
                        ins = nc.tensor.transpose((YD, YE)[half][:, c, :], xn[:, k * P:(k + 1) * P], ident)
                    ins.then_inc(*did(n))
                elif n == "lg":
                    pe.wait_ge(*at("hc1", t))
                    for k in range(KD):
                        ins = nc.tensor.matmul(YD[:, 0, :], hT[:, k, :], router[:, k, :],
                                               start=(k == 0), stop=(k == KD - 1))
                    ins.then_inc(*did(n))
                elif n == "rk":
                    pe.wait_ge(*at("vh", t, 0 if stream else -1))
                    pe.wait_ge(*at("r3", t))
                    nc.tensor.matmul(flat(YA)[:, 0:NE], mat("before"), OO[:, :], start=True, stop=True)
                    nc.tensor.matmul(flat(YA)[:, NE:2 * NE], mat("ones"), OO[:, :], start=True, stop=True
                                     ).then_inc(*did(n))

            pe.wait_ge(weights_in, 16 * 3)
            program("pe", pe, x_step, y_step)

        @block.scalar
        def _(act):
            def x_step(n, t, p, stream, did):
                if n == "sq":
                    act.wait_ge(ft_in[p], ft_turn(t, p))
                    act.wait_ge(*at("stat", t, 1))
                    nc.scalar.activation(sqb[:, :, :], ft[p][:, 0:2 * H, :], ACT.Square).then_inc(*did(n))
                elif n == "ex":
                    act.wait_ge(*at("o", t, 2))
                    act.wait_ge(*at("sc", t, 2))
                    act.wait_ge(*at("sse", t))
                    w = 3 * H + (SB * H if stream else 0)
                    nc.scalar.activation(ex[p][:, 0:w], flat(XB)[:, 2 * H:2 * H + w], ACT.Exp).then_inc(*did(n))
                elif n == "DT":
                    act.wait_ge(*at("AT", t, 1))
                    act.wait_ge(*at("dec", t))
                    nc.scalar.activation(DT[:, :, :], XA[:, :, :], ACT.Exp).then_inc(*did(n))
                elif n == "ktc":
                    act.wait_ge(*at("dS", t, 2))
                    act.wait_ge(*at("kt", t))
                    nc.scalar.activation(ktok[p][:, :, :], XC[:, :, :], ACT.Copy).then_inc(*did(n))
                elif n == "vs":
                    act.wait_ge(*at("X", t, 2))
                    act.wait_ge(*at("vt", t))
                    act.wait_ge(*at("sc", t))
                    for h in range(H):
                        ins = nc.scalar.activation(vs[p][:, h, :], XB[:, h, :], ACT.Copy, scale=sc[p][:, 0, h:h + 1])
                    ins.then_inc(*did(n))
                elif n == "T1c":
                    act.wait_ge(*at("Z64", t, 1))
                    act.wait_ge(*at("T1", t))
                    nc.scalar.activation(Tm[:, :, :], XA[:, :, :], ACT.Copy).then_inc(*did(n))
                elif n[0] == "T":
                    act.drain()
                    act.wait_ge(*at(n[:-1], t))
                    nc.scalar.activation(Tm[:, :, :], XC[:, :, :], ACT.Copy).then_inc(*did(n))
                elif n == "Z64c":
                    act.wait_ge(*at("N", t, 2))
                    act.wait_ge(*at("Z64", t))
                    nc.scalar.activation(Zf[p][:, :, :], XA[:, :, :], ACT.Copy).then_inc(*did(n))
                elif n[0] == "Z":
                    act.drain()
                    act.wait_ge(*at(n[:-1], t))
                    nc.scalar.activation(Zm[:, :, :], XA[:, :, :], ACT.Copy).then_inc(*did(n))

            def y_step(n, t, p, stream, did):
                if n == "o1":
                    act.wait_ge(*at("o", t, 1))
                    act.wait_ge(*at("QS", t))
                    for h in range(H):
                        ins = nc.scalar.activation(o1[:, h, :], YB[:, h, :], ACT.Copy, scale=ex[p][:, h:h + 1])
                    ins.then_inc(*did(n))
                elif n == "vh":
                    act.wait_ge(*at("N", t))
                    act.wait_ge(*at("vd", t))
                    for h in range(H):
                        ins = nc.scalar.activation(vhat[:, h, :], YA[:, h, :], ACT.Copy, scale=sc[p][:, 1, h:h + 1])
                    ins.then_inc(*did(n))
                elif n == "so":
                    act.drain()
                    act.wait_ge(*at("ro", t, 1))
                    act.wait_ge(*at("o", t))
                    for h in range(H):
                        if h:
                            act.drain()
                        ins = nc.scalar.activation(junk[:, 0:P], ob[:, h, :], ACT.Square, scale=sc[p][:, 6, h:h + 1],
                                                   accum_out=so[:, h:h + 1])
                    ins.then_inc(*did(n))
                elif n == "st":
                    act.drain()
                    act.wait_ge(*at("r2", t, 1))
                    act.wait_ge(*at("x2", t))
                    act.dma_start(T["x2"][bass.ts(t, P), :], x2b[:, :]).then_inc(x2_out, 16)
                    nc.scalar.activation(junk[:, :], x2b[:, :], ACT.Square, scale=D ** -0.5, accum_out=s2[:, :]
                                         ).then_inc(*did(n))
                elif n == "sh":
                    act.wait_ge(*at("h2", t))
                    act.dma_start(T["h2"][bass.ts(t, P), :], h2b[:, :]).then_inc(h2_out, 16)
                    act.sem_inc(*did(n))
                elif n == "rx":
                    act.wait_ge(*at("r1", t))
                    nc.scalar.activation(exd[:, 0:NGR], dif[:, 0:NGR], ACT.Exp, accum_out=sg[:, :])
                    nc.scalar.activation(exd[:, NGR:], dif[:, NGR:], ACT.Exp).then_inc(*did(n))

            program("act", act, x_step, y_step)

        @block.gpsimd
        def _(pool):
            nc.gpsimd.memset(neghalf[:, :], -0.5)
            nc.gpsimd.memset(eps[:, :], EPS)
            pool.drain()

            def x_step(n, t, p, stream, did):
                if n == "rr":
                    pool.wait_ge(*at("sc", t, 1))
                    pool.wait_ge(*at("sse", t))
                    nc.gpsimd.tensor_tensor(rr[:, :], sse[:, :], neghalf[:, :], ALU.pow).then_inc(*did(n))
                elif n == "ATm":
                    pool.wait_ge(*at("AT", t))
                    nc.gpsimd.tensor_tensor(AT[p][:, :, :], AT[p][:, :, :], heads(mat("upto_s" if stream else "upto")),
                                            ALU.mult).then_inc(*did(n))
                elif n[0] == "B":
                    s = int(n[1:])
                    pool.wait_ge(*at(f"W{s}", t, 1))
                    pool.wait_ge(*at("G", t))
                    nc.gpsimd.tensor_tensor(Bs[s][:, :, :], G[:, :, :], heads(mat(f"level{s}")), ALU.mult
                                            ).then_inc(*did(n))

            def y_step(n, t, p, stream, did):
                if n == "ro":
                    pool.wait_ge(*at("on", t, 1))
                    pool.wait_ge(*at("so", t))
                    nc.gpsimd.tensor_tensor(ro[:, :], so[:, :], eps[:, 0:H], ALU.add)
                    pool.drain()
                    nc.gpsimd.tensor_tensor(ro[:, :], ro[:, :], neghalf[:, 0:H], ALU.pow)
                    pool.drain()
                    nc.gpsimd.tensor_tensor(ro[:, :], ro[:, :], sc[p][:, 3, :], ALU.mult).then_inc(*did(n))
                elif n == "r2":
                    pool.wait_ge(*at("xn", t, 1))
                    pool.wait_ge(*at("st", t))
                    nc.gpsimd.tensor_tensor(rs2[:, :], s2[:, :], eps[:, 0:1], ALU.add)
                    pool.drain()
                    nc.gpsimd.tensor_tensor(rs2[:, :], rs2[:, :], neghalf[:, 0:1], ALU.pow).then_inc(*did(n))
                elif n == "h2":
                    pool.wait_ge(h2_out, 16 * (t + 1))
                    pool.wait_ge(*at("xn", t))
                    nc.gpsimd.tensor_tensor(h2b[:, :], xn[:, :], ln2_row[:, :], ALU.mult).then_inc(*did(n))
                elif n == "sct":
                    pool.wait_ge(*at("off", t))
                    for k in range(2):
                        if k:
                            pool.wait_ge(ids_out, 32 * t + 16)
                        pool.sem_inc(scatters, 1)
                        pool.indirect_dma_start(T["table"], bass.IndirectOffsetOnAxis(ap=offs[k][:, 0:1], axis=0),
                                                tid[:, 0:1], None).then_inc(ids_out, 16)
                    pool.wait_ge(ids_out, 32 * t + 32)
                    pool.sem_inc(*did(n))

            pool.wait_ge(weights_in, 16 * 3)
            pool.sem_inc(h2_out, 16)
            program("pool", pool, x_step, y_step)
            pool.wait_ge(h2_out, 16 * (NT + 1))
            pool.wait_ge(x2_out, 16 * (NT + 1))

        @block.vector
        def _(dve):
            def x_step(n, t, p, stream, did):
                if n == "gs":
                    dve.wait_ge(*at("dec", t, 1))
                    nc.vector.tensor_copy(gt[p][:, :], gb[:, bass.ds(t, 1), :].rearrange("p a b -> p (a b)"))
                    dve.drain()
                    nc.vector.tensor_copy(gw[:, 0:H], gt[p][:, H:])
                    for h in range(H):
                        ins = nc.vector.tensor_scalar(gs[:, h, :], mat("after_s" if stream else "after"),
                                                      gt[p][:, H + h:H + h + 1], None, ALU.mult)
                    if stream:
                        ins = nc.vector.tensor_tensor(
                            gsel[:, :, :], gt[p][:, H:].unsqueeze(1).to_broadcast([P, SB, H]),
                            col("stream", 0, SB).unsqueeze(2).to_broadcast([P, SB, H]), ALU.mult)
                    ins.then_inc(*did(n))
                elif n == "sse":
                    dve.drain()
                    dve.wait_ge(*at("rr", t, 1))
                    dve.wait_ge(*at("stat", t))
                    nc.vector.tensor_scalar(sse[:, :], flat(XB)[:, 0:2 * H], EPS, None, ALU.add).then_inc(*did(n))
                elif n == "sc":
                    c = sc[p]
                    dve.wait_ge(*at("ro", t, 2))
                    dve.wait_ge(*at("vh", t, 2))
                    dve.wait_ge(*at("ex", t))
                    dve.wait_ge(*at("rr", t))
                    nc.vector.tensor_tensor(c[:, 0, :], sse[:, H:], rr[:, H:], ALU.mult)
                    nc.vector.tensor_tensor(c[:, 5, :], rr[:, H:], rr[:, H:], ALU.mult)
                    nc.vector.tensor_scalar(c[:, 2, :], ex[p][:, 0:H], -1.0, None, ALU.mult)
                    nc.vector.tensor_scalar(c[:, 3, :], rr[:, 0:H], P ** -0.5, None, ALU.mult)
                    nc.vector.tensor_scalar(c[:, 6, :], rr[:, 0:H], 1.0 / P, None, ALU.mult)
                    dve.drain()
                    nc.vector.tensor_tensor(c[:, 1, :], c[:, 5, :], gt[p][:, 0:H], ALU.mult)
                    dve.drain()
                    nc.vector.tensor_tensor(c[:, 4, :], c[:, 1, :], ex[p][:, H:2 * H], ALU.mult).then_inc(*did(n))
                elif n == "G":
                    dve.wait_ge(*at("B64", t, 1))
                    dve.wait_ge(*at("DT", t))
                    dve.wait_ge(*at("KK", t))
                    for h in range(H):
                        ins = nc.vector.scalar_tensor_tensor(G[:, h, :], XA[:, h, :], sc[p][:, 1, h:h + 1], DT[:, h, :],
                                                             ALU.mult, ALU.mult)
                    if stream:
                        dve.drain()
                        ins = nc.vector.tensor_tensor(G[:, :, :], G[:, :, :], heads(mat("upto_s")), ALU.mult)
                    ins.then_inc(*did(n))
                elif n == "AT":
                    dve.wait_ge(*at("AV", t, 2))
                    dve.wait_ge(*at("QK", t))
                    nc.vector.tensor_tensor(AT[p][:, :, :], XC[:, :, :], DT[:, :, :], ALU.mult).then_inc(*did(n))
                elif n == "Z1":
                    dve.drain()
                    dve.wait_ge(*at("Z64", t, 1))
                    nc.vector.tensor_tensor(Bs[1][:, :, :], G[:, :, :], heads(mat("level1")), ALU.mult)
                    dve.drain()
                    nc.vector.tensor_tensor(Zm[:, :, :], Bs[1][:, :, :], heads(mat("ident")), ALU.add).then_inc(*did(n))
                elif n[0] == "I":
                    dve.wait_ge(*at(f"W{n[1:]}", t))
                    nc.vector.tensor_tensor(WI[:, :, :], XB[:, :, :], heads(mat("ident")), ALU.add).then_inc(*did(n))
                if n == "I64" and stream:
                    nc.vector.memset(kz[:, :, :, :], 0.0)
                    dve.drain()
                    for b in range(SB):
                        r = slice(b * SL, (b + 1) * SL)
                        ins = nc.vector.tensor_copy(kz[:, :, b, r], ft[p][:, H:2 * H, r])
                    ins.then_inc(spread, 1)

            def y_step(n, t, p, stream, did):
                if n == "X" and stream:
                    dve.wait_ge(*at("KS", t))
                    for b in range(SB):
                        r = slice(b * SL, (b + 1) * SL)
                        ins = nc.vector.tensor_copy(kz[:, :, b, r], ft[p][:, 0:H, r])
                    ins.then_inc(spread, 1)
                if n == "X":
                    dve.wait_ge(*at("vs", t))
                    dve.wait_ge(*at("KS", t))
                    for h in range(H):
                        ins = nc.vector.scalar_tensor_tensor(xb[:, h, :], YA[:, h, :], sc[p][:, 2, h:h + 1], vs[p][:, h, :],
                                                             ALU.mult, ALU.add)
                    ins.then_inc(*did(n))
                elif n == "vd":
                    dve.wait_ge(*at("N", t))
                    nc.vector.tensor_tensor(vdec[:, :, :], YA[:, :, :], per_head(sc[p][:, 4, :]), ALU.mult
                                            ).then_inc(*did(n))
                    if stream:
                        for b in range(SB):
                            if b == 0:
                                dve.drain()
                            else:
                                dve.wait_ge(stream_mm, b)
                            nc.vector.tensor_scalar(vm[:, :, :], vdec[:, :, :], col("stream", b), None, ALU.mult
                                                    ).then_inc(vm_ready, 1)
                            dve.wait_ge(stream_mm, b + 1)
                            for h in range(H):
                                e = 3 * H + b * H + h
                                ins = nc.vector.scalar_tensor_tensor(S_s[:, b, h, :], S_s[:, b, h, :], ex[p][:, e:e + 1],
                                                                     YC[:, h, :], ALU.mult, ALU.add)
                            ins.then_inc(stream_S, 1)
                elif n == "S":
                    dve.wait_ge(*at("dS", t))
                    if stream:
                        nc.vector.tensor_copy(vm[:, 0, 0:1], YC[:, 0, 0:1]).then_inc(*did(n))
                    else:
                        for h in range(H):
                            ins = nc.vector.scalar_tensor_tensor(S[:, h, :], S[:, h, :], ex[p][:, 2 * H + h:2 * H + h + 1],
                                                                 YC[:, h, :], ALU.mult, ALU.add)
                        ins.then_inc(*did(n))
                elif n == "o":
                    dve.wait_ge(*at("so", t, 1))
                    dve.wait_ge(*at("o1", t))
                    dve.wait_ge(*at("AV", t))
                    nc.vector.tensor_tensor(ob[:, :, :], YB[:, :, :], o1[:, :, :], ALU.add).then_inc(*did(n))
                elif n == "on":
                    dve.wait_ge(*at("oT", t, 1))
                    dve.wait_ge(*at("ro", t))
                    nc.vector.tensor_tensor(onb[:, :, :], ob[:, :, :], per_head(ro[:, :]), ALU.mult).then_inc(*did(n))
                elif n == "mx":
                    dve.wait_ge(*at("oT", t))
                    nc.vector.scalar_tensor_tensor(mx[:, :, :], YC[:, :, :], col("ng"), ft[p][:, QC:QC + ZC, :],
                                                   ALU.mult, ALU.mult).then_inc(*did(n))
                elif n == "x2":
                    dve.wait_ge(xr_in[p], ft_turn(t, p))
                    dve.wait_ge(x2_out, 16 * (t + 1))
                    dve.wait_ge(*at("st", t, 1))
                    dve.wait_ge(*at("outB7", t))
                    nc.vector.tensor_tensor(x2b[:, 0:512], flat(YD), xr[p][:, 0:512], ALU.add)
                    nc.vector.tensor_tensor(x2b[:, 512:], flat(YE), xr[p][:, 512:], ALU.add).then_inc(*did(n))
                elif n == "xn":
                    dve.wait_ge(*at("h2", t, 1))
                    dve.wait_ge(*at("hT1", t, 1))
                    dve.wait_ge(*at("r2", t))
                    nc.vector.tensor_scalar(xn[:, :], x2b[:, :], rs2[:, 0:1], None, ALU.mult).then_inc(*did(n))
                elif n in ("hc0", "hc1"):
                    half = int(n[-1])
                    dve.wait_ge(*at(f"hT{half}", t))
                    nc.vector.tensor_tensor(hT[:, 4 * half:4 * half + 4, :], (YD, YE)[half][:, :, :],
                                            per_head(col("ln2", 4 * half, 4)), ALU.mult).then_inc(*did(n))
                elif n == "r0":
                    dve.drain()
                    dve.wait_ge(*at("lg", t))
                    nc.vector.tensor_tensor(gpad[:, 0:NGR], flat(YD)[:, 0:NGR], col("rb", 0, NGR), ALU.add)
                    nc.vector.tensor_tensor(lg[:, :], flat(YD)[:, NGR:NGR + NE], col("rb", NGR, NE), ALU.add
                                            ).then_inc(*did(n))
                elif n == "r1":
                    dve.drain()
                    nc.vector.max(m8[:, :], gpad[:, :])
                    dve.drain()
                    nc.vector.max_index(i8[:, :], m8[:, :], gpad[:, :])
                    dve.drain()
                    nc.vector.tensor_copy(gid[:, :], i8[:, 0:1])
                    dve.drain()
                    nc.vector.tensor_scalar(goh[:, :], col("iota", 0, NGR), gid[:, 0:1], None, ALU.is_equal)
                    nc.vector.tensor_scalar(gid8[:, :], gid[:, :], float(EPG), None, ALU.mult)
                    dve.drain()
                    nc.vector.tensor_scalar(esel[:, :], lg[:, 0:EPG], goh[:, 0:1], None, ALU.mult)
                    for g in range(1, NGR):
                        dve.drain()
                        nc.vector.scalar_tensor_tensor(esel[:, :], lg[:, g * EPG:(g + 1) * EPG], goh[:, g:g + 1], esel[:, :],
                                                       ALU.mult, ALU.add)
                    dve.drain()
                    nc.vector.max(m8e[:, :], esel[:, :])
                    dve.drain()
                    nc.vector.max_index(i8e[:, :], m8e[:, :], esel[:, :])
                    dve.wait_ge(*at("rx", t, 1))
                    nc.vector.tensor_scalar(dif[:, 0:NGR], gpad[:, 0:NGR], m8[:, 0:1], None, ALU.subtract)
                    nc.vector.tensor_tensor(dif[:, NGR:], m8e[:, 1:2], m8e[:, 0:1], ALU.subtract).then_inc(*did(n))
                elif n == "r3":
                    dve.wait_ge(*at("rx", t))
                    nc.vector.scalar_tensor_tensor(den[:, :], exd[:, NGR:], 1.0, sg[:, :], ALU.add, ALU.mult)
                    nc.vector.tensor_copy(ief[:, :], i8e[:, 0:2])
                    dve.drain()
                    nc.vector.reciprocal(w2t[:, 0:1], den[:, :])
                    nc.vector.tensor_scalar(e2[:, :], ief[:, :], gid8[:, 0:1], None, ALU.add)
                    dve.drain()
                    nc.vector.tensor_tensor(w2t[:, 1:2], w2t[:, 0:1], exd[:, NGR:], ALU.mult)
                    dve.wait_ge(*at("rk", t, 1))
                    nc.vector.tensor_scalar(O0[:, :], col("iota", 0, NE), e2[:, 0:1], None, ALU.is_equal)
                    nc.vector.tensor_scalar(O1[:, :], col("iota", 0, NE), e2[:, 1:2], None, ALU.is_equal)
                    dve.drain()
                    nc.vector.tensor_tensor(OO[:, :], O0[:, :], O1[:, :], ALU.add).then_inc(*did(n))
                    nc.vector.tensor_copy(wts[:, bass.ds(t, 1), :].rearrange("p a b -> p (a b)"), w2t[:, :])
                    nc.vector.tensor_copy(eid[:, bass.ds(t, 1), :].rearrange("p a b -> p (a b)"), e2[:, :])
                elif n == "off":
                    dve.wait_ge(*at("sct", t, 1))
                    dve.wait_ge(*at("rk", t))
                    old, new = base[:, 0, :], base[:, 1, :]
                    nc.vector.tensor_tensor(rkf[:, :], flat(YA)[:, 0:NE], old, ALU.add)
                    nc.vector.tensor_tensor(new, flat(YA)[:, NE:2 * NE], old, ALU.add)
                    nc.vector.tensor_copy(tid[:, :], tok[:, bass.ds(t, 1)])
                    dve.drain()
                    nc.vector.tensor_copy(old, new)
                    nc.vector.scalar_tensor_tensor(rjunk[:, :], rkf[:, :], 1.0, O0[:, :], ALU.mult, ALU.mult,
                                                   accum_out=r2t[:, 0:1])
                    dve.drain()
                    nc.vector.scalar_tensor_tensor(rjunk[:, :], rkf[:, :], 1.0, O1[:, :], ALU.mult, ALU.mult,
                                                   accum_out=r2t[:, 1:2])
                    dve.drain()
                    nc.vector.tensor_copy(rank[:, bass.ds(t, 1), :].rearrange("p a b -> p (a b)"), r2t[:, :])
                    for k in range(2):
                        ins = nc.vector.scalar_tensor_tensor(offs[k][:, :], e2[:, k:k + 1], float(NT * P), r2t[:, k:k + 1],
                                                             ALU.mult, ALU.add)
                    ins.then_inc(*did(n))

            nc.vector.memset(S[:, :, :], 0.0)
            nc.vector.memset(gw[:, :], 0.0)
            nc.vector.memset(base[:, :, :], 0.0)
            nc.vector.memset(gpad[:, :], -1e30)
            dve.sem_inc(x2_out, 16)
            dve.drain()
            program("dve", dve, x_step, y_step)
            dve.drain()
            nc.vector.tensor_copy(rjunk[:, 0:1], S[:, 0, 0:1]).then_inc(S_ready, 2)


EXPERTS = """
M.up.pe M.silu.act M.mul.dve
O.gT.pe O.gTc.act
T.T0.pe T.T1.pe T.T0c.act T.T1c.dve
O.d0.pe O.d1.pe O.d0c.act O.d1c.dve O.st.act
""".split()
EXPERTS = [tuple(s.split(".")) for s in EXPERTS]


def load_expert(engine, T, weights, e, p):
    w13, w2, loaded = weights
    for dst, src in ((w13, "w13"), (w2, "w2")):
        engine.dma_start(dst[:, p, :], T[src][bass.ds(e, 1)].rearrange("a p n -> p (a n)")).then_inc(loaded[p], 16)


def routing_phase(nc, T, cols, eid, rank, base, dest, tabs, weights):
    NT, NB = tiles(), blocks()
    with ExitStack() as ctx:
        def sb(name, shape, dt=FP32):
            return ctx.enter_context(nc.sbuf_tensor(name, shape, dt))

        cnt = sb("cnt", [P, NE], I32)
        nb = sb("nb", [P, NE])
        ones = sb("ones_r", [P, NE])
        end = sb("end", [P, NE])
        start = sb("start", [P, NE])
        hot = sb("hot", [P, 2 * NT, NE])
        first = sb("first", [P, 2 * NT])
        bi = sb("bi", [1, NB])
        past = sb("past", [1, NB, NE])
        be = sb("be", [1, NB])
        bs = sb("bs", [1, NB])
        lst = sb("lst", [1, NB])
        valid = sb("valid", [1, NB])
        bi_in = ctx.enter_context(nc.semaphore("bi_in"))
        block = ctx.enter_context(nc.Block())

        @block.sync
        def _(sp):
            sp.dma_start(bi[:, :], T["block_iota"]).then_inc(bi_in, 16)
            for p in range(2):
                load_expert(sp, T, weights, p, p)

        @block.vector
        def _(dve):
            v = nc.vector
            iota = cols[:, COLS["iota"][0]:COLS["iota"][1]]
            v.tensor_scalar(cnt[:, :], base[:, 0, :], float(P - 1), None, ALU.add)
            v.memset(ones[:, :], 1.0)
            dve.drain()
            v.tensor_scalar(cnt[:, :], cnt[:, :], 7, None, ALU.logical_shift_right)
            dve.drain()
            v.tensor_copy(nb[:, :], cnt[:, :])
            dve.drain()
            v.tensor_tensor_scan(end[:, :], ones[:, :], nb[:, :], 0.0, ALU.mult, ALU.add)
            dve.drain()
            v.tensor_tensor(start[:, :], end[:, :], nb[:, :], ALU.subtract)
            dve.drain()
            v.tensor_scalar(start[:, :], start[:, :], float(P), None, ALU.mult)
            v.tensor_tensor(hot[:, :, :], eid[:, :, :].rearrange("p t k -> p (t k)").unsqueeze(2).to_broadcast([P, 2 * NT, NE]),
                            iota.unsqueeze(1).to_broadcast([P, 2 * NT, NE]), ALU.is_equal)
            dve.drain()
            v.tensor_tensor(hot[:, :, :], hot[:, :, :], start[:, :].unsqueeze(1).to_broadcast([P, 2 * NT, NE]), ALU.mult)
            dve.drain()
            v.reduce_sum(first[:, :], hot[:, :, :], AX.X)
            dve.drain()
            v.tensor_tensor(dest[:, :], first[:, :], rank[:, :, :].rearrange("p t k -> p (t k)"), ALU.add)
            dve.wait_ge(bi_in, 16)
            v.tensor_tensor(past[:, :, :], bi[:, :].unsqueeze(2).to_broadcast([1, NB, NE]),
                            end[0:1, :].unsqueeze(1).to_broadcast([1, NB, NE]), ALU.is_ge)
            dve.drain()
            v.reduce_sum(be[:, :], past[:, :, :], AX.X)
            dve.drain()
            v.tensor_tensor(past[:, :, :], past[:, :, :], nb[0:1, :].unsqueeze(1).to_broadcast([1, NB, NE]), ALU.mult)
            v.tensor_scalar(be[:, :], be[:, :], float(NE - 1), None, ALU.min)
            dve.drain()
            v.reduce_sum(bs[:, :], past[:, :, :], AX.X)
            v.tensor_scalar(valid[:, :], bi[:, :], end[0:1, NE - 1:NE], None, ALU.is_lt)
            v.tensor_copy(tabs["expert"][:, :], be[:, :])
            v.tensor_copy(tabs["end"][:, :], end[0:1, :])
            dve.drain()
            v.tensor_tensor(bs[:, :], bi[:, :], bs[:, :], ALU.subtract)
            v.tensor_scalar(lst[:, :], be[:, :], float(NT * P), -float(NE * NT * P), ALU.mult, ALU.add)
            v.tensor_scalar(tabs["slot"][:, :], tabs["expert"][:, :], 1, None, ALU.bitwise_and)
            dve.drain()
            v.scalar_tensor_tensor(lst[:, :], bs[:, :], float(P), lst[:, :], ALU.mult, ALU.add)
            dve.drain()
            v.tensor_tensor(lst[:, :], lst[:, :], valid[:, :], ALU.mult)
            dve.drain()
            v.tensor_scalar(tabs["list"][:, :], lst[:, :], float(NE * NT * P), None, ALU.add)


def experts_phase(nc, T, const, tabs, weights):
    NT, NB = tiles(), blocks()
    with ExitStack() as ctx:
        def sb(name, shape, dt=FP32):
            return ctx.enter_context(nc.sbuf_tensor(name, shape, dt))

        def sem(name):
            return ctx.enter_context(nc.semaphore(name))

        w13, w2, loaded = weights
        idx = [sb(f"idx{p}", [P, 1], I32) for p in range(2)]
        xb = [sb(f"rows{p}", [P, D]) for p in range(2)]
        xT = [sb(f"rowsT{p}", [P, KD, P]) for p in range(2)]
        sil = [sb(f"sil{p}", [P, FE]) for p in range(2)]
        gu = [sb(f"gu{p}", [P, FE]) for p in range(2)]
        guT = [sb(f"guT{p}", [P, FE // P, P]) for p in range(2)]
        yb = [sb(f"yb{p}", [P, D]) for p in range(2)]
        TA, TB, M0, M1, GB, OA, OB = [ctx.enter_context(nc.psum_tensor(f"ebank{n}", [P, 512], FP32)) for n in range(7)]

        done = {(st, e): Steps(sem(f"experts_{st}_{e}"), [n for a, n, b in EXPERTS if a == st and b == e], lead=2)
                for st in "TMO" for e in ("pe", "act", "dve") if any(a == st and b == e for a, n, b in EXPERTS)}
        owner = {n: done[st, e] for st, n, e in EXPERTS}
        ready = sem("expert_ready")
        idx_in = [sem(f"idx_in{p}") for p in range(2)]
        rows_in = [sem(f"rows_in{p}") for p in range(2)]
        y_out = [sem(f"y_out{p}") for p in range(2)]
        gathers = sem("gathers")

        def at(name, t, back=0):
            return owner[name].at(name, t, back)

        def turn(b, p):
            return (b - p) * 8 + 16

        def program(engine, begin, step):
            for key, d in done.items():
                if key[1] == engine:
                    d.begin(begin)

            def run(bt, bm, bo):
                for st, n, e in EXPERTS:
                    b = {"T": bt, "M": bm, "O": bo}[st]
                    if e == engine and b is not None:
                        step(n, b[0], b[1], done[st, e].did)

            run((0, 0), None, None)
            run((1, 1), (0, 0), None)
            with begin.Fori(0, (NB - 2) // 2) as pair:
                b = pair * 2
                run((b + 2, 0), (b + 1, 1), (b, 0))
                run((b + 3, 1), (b + 2, 0), (b + 1, 1))
            run(None, (NB - 1, 1), (NB - 2, 0))
            run(None, None, (NB - 1, 1))

        block = ctx.enter_context(nc.Block())

        @block.sync
        def _(sp):
            def arrived(e, p):
                sp.wait_ge(loaded[p], (e - p) * 16 + 32)
                sp.sem_inc(ready, 1)

            arrived(0, 0)
            arrived(1, 1)
            with sp.Fori(0, (NE - 2) // 2) as pair:
                for p in range(2):
                    end = sp.value_load(tabs["end"][0:1, bass.ds(pair * 2 + p, 1)], min_val=0, max_val=NB)
                    sem_, value = at("d1", end, 1)
                    sp.wait_ge(sem_, value)
                    load_expert(sp, T, weights, pair * 2 + (2 + p), p)
                    arrived(pair * 2 + (2 + p), p)

        @block.gpsimd
        def _(pool):
            def fetch(b, p):
                where = pool.value_load(tabs["list"][0:1, bass.ds(b, 1)], min_val=0, max_val=NE * NT * P)
                pool.wait_ge(*at("T1", b, 2))
                pool.dma_start(idx[p][:, :], T["table"][bass.ds(where, P), :]).then_inc(idx_in[p], 16)
                pool.wait_ge(idx_in[p], turn(b, p))
                pool.sem_inc(gathers, 1)
                pool.indirect_dma_start(xb[p][:, :], None, T["h2"], bass.IndirectOffsetOnAxis(ap=idx[p][:, 0:1], axis=0)
                                        ).then_inc(rows_in[p], 16)

            with pool.Fori(0, NB // 2) as pair:
                fetch(pair * 2, 0)
                fetch(pair * 2 + 1, 1)

        @block.tensor
        def _(pe):
            ident = const[:, MATS.index("ident"), :]

            def step(n, b, p, did):
                if n in ("T0", "T1"):
                    h = int(n[1])
                    bank = (TA, TB)[h]
                    pe.wait_ge(*at("T0c" if h == 0 else "T1c", b, 1))
                    pe.wait_ge(rows_in[p], turn(b, p))
                    for k in range(4):
                        c = 4 * h + k
                        ins = nc.tensor.transpose(bank[:, k * P:(k + 1) * P], xb[p][:, c * P:(c + 1) * P], ident)
                    ins.then_inc(*did(n))
                elif n == "up":
                    e = pe.value_load(tabs["expert"][0:1, bass.ds(b, 1)], min_val=0, max_val=NE - 1)
                    s = pe.value_load(tabs["slot"][0:1, bass.ds(b, 1)], min_val=0, max_val=1)
                    pe.wait_ge(ready, e + 1)
                    pe.wait_ge(*at("mul", b, 2))
                    pe.wait_ge(*at("T0c", b))
                    pe.wait_ge(*at("T1c", b))
                    for k in range(KD):
                        ins = nc.tensor.matmul((M0, M1)[p][:, :], xT[p][:, k, :],
                                               w13[:, bass.ds(s, 1), k * 512:(k + 1) * 512].rearrange("p a n -> p (a n)"),
                                               start=(k == 0), stop=(k == KD - 1))
                    ins.then_inc(*did(n))
                elif n == "gT":
                    pe.wait_ge(*at("gTc", b, 1))
                    pe.wait_ge(*at("mul", b))
                    for k in range(FE // P):
                        ins = nc.tensor.transpose(GB[:, k * P:(k + 1) * P], gu[p][:, k * P:(k + 1) * P], ident)
                    ins.then_inc(*did(n))
                elif n in ("d0", "d1"):
                    h = int(n[1])
                    if h == 0:
                        pe_slot[0] = pe.value_load(tabs["slot"][0:1, bass.ds(b, 1)], min_val=0, max_val=1)
                    pe.wait_ge(*at("d0c" if h == 0 else "d1c", b, 1))
                    pe.wait_ge(*at("gTc", b))
                    for k in range(FE // P):
                        w = w2[:, bass.ds(pe_slot[0], 1), k * D + h * 512:k * D + h * 512 + 512]
                        ins = nc.tensor.matmul((OA, OB)[h][:, :], guT[p][:, k, :], w.rearrange("p a n -> p (a n)"),
                                               start=(k == 0), stop=(k == FE // P - 1))
                    ins.then_inc(*did(n))

            pe_slot = [None]
            program("pe", pe, step)

        @block.scalar
        def _(act):
            def step(n, b, p, did):
                if n == "T0c":
                    act.wait_ge(*at("up", b, 2))
                    act.wait_ge(*at("T0", b))
                    nc.scalar.activation(xT[p][:, 0:4, :].rearrange("p k n -> p (k n)"), TA[:, :], ACT.Copy).then_inc(*did(n))
                elif n == "silu":
                    act.wait_ge(*at("mul", b, 2))
                    act.wait_ge(*at("up", b))
                    nc.scalar.activation(sil[p][:, :], (M0, M1)[p][:, 0:FE], ACT.Silu).then_inc(*did(n))
                elif n == "gTc":
                    act.wait_ge(*at("d1", b, 2))
                    act.wait_ge(*at("gT", b))
                    nc.scalar.activation(guT[p][:, :, :].rearrange("p k n -> p (k n)"), GB[:, 0:FE], ACT.Copy
                                         ).then_inc(*did(n))
                elif n == "d0c":
                    act.wait_ge(y_out[p], turn(b, p))
                    act.wait_ge(*at("d0", b))
                    nc.scalar.activation(yb[p][:, 0:512], OA[:, :], ACT.Copy).then_inc(*did(n))
                elif n == "st":
                    act.wait_ge(*at("d0c", b))
                    act.wait_ge(*at("d1c", b))
                    act.dma_start(T["y"][bass.ts(b, P), :], yb[p][:, :]).then_inc(y_out[p], 16)
                    act.sem_inc(*did(n))

            for p in range(2):
                act.sem_inc(y_out[p], 16)
            program("act", act, step)
            for p in range(2):
                act.wait_ge(y_out[p], NB // 2 * 16 + 16)

        @block.vector
        def _(dve):
            def step(n, b, p, did):
                if n == "T1c":
                    dve.wait_ge(*at("up", b, 2))
                    dve.wait_ge(*at("T1", b))
                    nc.vector.tensor_copy(xT[p][:, 4:8, :].rearrange("p k n -> p (k n)"), TB[:, :]).then_inc(*did(n))
                elif n == "mul":
                    dve.wait_ge(*at("gT", b, 2))
                    dve.wait_ge(*at("silu", b))
                    nc.vector.tensor_tensor(gu[p][:, :], (M0, M1)[p][:, FE:2 * FE], sil[p][:, :], ALU.mult
                                            ).then_inc(*did(n))
                elif n == "d1c":
                    dve.wait_ge(y_out[p], turn(b, p))
                    dve.wait_ge(*at("d1", b))
                    nc.vector.tensor_copy(yb[p][:, 512:], OB[:, :]).then_inc(*did(n))

            program("dve", dve, step)


def combine_phase(nc, T, dest, wts):
    NT = tiles()
    with ExitStack() as ctx:
        def sb(name, shape, dt=FP32):
            return ctx.enter_context(nc.sbuf_tensor(name, shape, dt))

        def sem(name):
            return ctx.enter_context(nc.semaphore(name))

        NS = 2
        final_row = sb("final_row", [P, D])
        at_row = [[sb(f"at_row{s}_{k}", [P, 1], I32) for k in range(2)] for s in range(NS)]
        yr = [[sb(f"yr{s}_{k}", [P, D]) for k in range(2)] for s in range(NS)]
        xx = [sb(f"xx{s}", [P, D]) for s in range(NS)]
        yo = [sb(f"yo{s}", [P, D]) for s in range(NS)]
        zo = [sb(f"zo{s}", [P, D]) for s in range(NS)]
        junk = sb("junk3", [P, D])
        ss = [sb(f"ss3_{s}", [P, 1]) for s in range(NS)]
        rs = [sb(f"rs3_{s}", [P, 1]) for s in range(NS)]
        neghalf = sb("neghalf3", [P, 1])
        eps = sb("eps3", [P, 1])
        ms = [sb(f"ms3_{s}", [P, 1]) for s in range(NS)]
        row_in = sem("row_in")
        eps_set = sem("eps_set")
        x_in = [sem(f"x2_in{s}") for s in range(NS)]
        y_in = [sem(f"y_in{s}") for s in range(NS)]
        out_done = [sem(f"out_done{s}") for s in range(NS)]
        gathers = sem("y_gathers")
        done = {n: Steps(sem(f"combine_{n}"), [n], lead=2) for n in ("rows", "sum", "ss", "ms", "rs", "out")}
        block = ctx.enter_context(nc.Block())

        def at(n, t, back=0):
            return done[n].at(n, t, back)

        def did(n):
            return done[n].did(n)

        def turn(t, p):
            return (t - p) * 8 + 16

        def every(engine, step):
            with engine.Fori(0, NT // 2) as pair:
                step(pair * 2, 0)
                step(pair * 2 + 1, 1)
            step(NT - 1, 0)

        @block.sync
        def _(sp):
            sp.dma_start(final_row[:, :], T["final_row"].to_broadcast([P, D])).then_inc(row_in, 16)

            def step(t, p):
                sp.wait_ge(*at("sum", t, 2))
                sp.dma_start(xx[p][:, :], T["x2"][bass.ts(t, P), :]).then_inc(x_in[p], 16)

            every(sp, step)

        @block.gpsimd
        def _(pool):
            done["rs"].begin(pool)
            nc.gpsimd.memset(neghalf[:, :], -0.5)
            nc.gpsimd.memset(eps[:, :], EPS).then_inc(eps_set, 1)
            pool.drain()

            def gather(t, p):
                pool.wait_ge(*at("sum", t, 2))
                pool.wait_ge(*at("rows", t))
                pool.sem_inc(gathers, 1)
                for k in range(2):
                    pool.indirect_dma_start(yr[p][k][:, :], None, T["y"],
                                            bass.IndirectOffsetOnAxis(ap=at_row[p][k][:, 0:1], axis=0)).then_inc(y_in[p], 16)

            def scale(t, p):
                pool.wait_ge(*at("out", t, 2))
                pool.wait_ge(*at("ms", t))
                nc.gpsimd.tensor_tensor(rs[p][:, :], ms[p][:, :], neghalf[:, :], ALU.pow).then_inc(*did("rs"))

            gather(0, 0)
            gather(1, 1)
            with pool.Fori(0, NT // 2 - 1) as pair:
                gather(pair * 2 + 2, 0)
                scale(pair * 2, 0)
                gather(pair * 2 + 3, 1)
                scale(pair * 2 + 1, 1)
            gather(NT - 1, 0)
            scale(NT - 3, 0)
            scale(NT - 2, 1)
            scale(NT - 1, 0)

        @block.scalar
        def _(act):
            done["ss"].begin(act)
            done["ms"].begin(act)
            act.wait_ge(eps_set, 1)

            def step(t, p):
                act.drain()
                act.wait_ge(*at("rs", t, 2))
                act.wait_ge(*at("sum", t))
                nc.scalar.activation(junk[:, :], yo[p][:, :], ACT.Square, scale=D ** -0.5, accum_out=ss[p][:, :]
                                     ).then_inc(*did("ss"))
                act.drain()
                nc.scalar.activation(ms[p][:, :], ss[p][:, :], ACT.Identity, bias=eps[:, 0:1]).then_inc(*did("ms"))

            def store(t, p):
                act.wait_ge(*at("out", t))
                act.dma_start(T["out_y"][bass.ts(t, P), :], zo[p][:, :]).then_inc(out_done[p], 16)

            for p in range(NS):
                act.sem_inc(out_done[p], 16)
            step(0, 0)
            with act.Fori(0, NT // 2) as pair:
                step(pair * 2 + 1, 1)
                store(pair * 2, 0)
                step(pair * 2 + 2, 0)
                store(pair * 2 + 1, 1)
            store(NT - 1, 0)
            act.wait_ge(out_done[0], 16 * ((NT + 1) // 2 + 1))
            act.wait_ge(out_done[1], 16 * (NT // 2 + 1))

        @block.vector
        def _(dve):
            for n in ("rows", "sum", "out"):
                done[n].begin(dve)

            def rows(t, p):
                for k in range(2):
                    ins = nc.vector.tensor_copy(at_row[p][k][:, :], dest[:, bass.ds(t * 2 + k, 1)])
                ins.then_inc(*did("rows"))

            def weight(t, k):
                return wts[:, bass.ds(t, 1), k:k + 1].rearrange("p a b -> p (a b)")

            def total(t, p):
                dve.wait_ge(*at("ss", t, 2))
                dve.wait_ge(x_in[p], turn(t, p))
                dve.wait_ge(y_in[p], (t - p) * 16 + 32)
                nc.vector.scalar_tensor_tensor(yo[p][:, :], yr[p][0][:, :], weight(t, 0), xx[p][:, :], ALU.mult, ALU.add)
                dve.drain()
                nc.vector.scalar_tensor_tensor(yo[p][:, :], yr[p][1][:, :], weight(t, 1), yo[p][:, :], ALU.mult, ALU.add
                                               ).then_inc(*did("sum"))

            def out(t, p):
                dve.drain()
                dve.wait_ge(out_done[p], turn(t, p))
                dve.wait_ge(*at("rs", t))
                nc.vector.scalar_tensor_tensor(zo[p][:, :], yo[p][:, :], rs[p][:, 0:1], final_row[:, :], ALU.mult, ALU.mult
                                               ).then_inc(*did("out"))

            def pair_of(t, following):
                rows(t + 2, 0)
                total(t + 1, 1)
                out(t, 0)
                if following:
                    rows(t + 3, 1)
                dve.drain()
                total(t + 2, 0)
                out(t + 1, 1)
                dve.drain()

            dve.wait_ge(row_in, 16)
            rows(0, 0)
            rows(1, 1)
            total(0, 0)
            with dve.Fori(0, NT // 2 - 1) as pair:
                pair_of(pair * 2, True)
            pair_of(NT - 3, False)
            out(NT - 1, 0)


def build(nc, T):
    with ExitStack() as ctx:
        gb = ctx.enter_context(nc.sbuf_tensor("gb", [P, tiles(), 2 * HEADS], FP32))
        const = ctx.enter_context(nc.sbuf_tensor("const", [P, NMAT, P], FP32))
        cols = ctx.enter_context(nc.sbuf_tensor("cols_sb", [P, NCOL], FP32))
        project_phase(nc, T, gb, const, cols)
        eid = ctx.enter_context(nc.sbuf_tensor("eid", [P, tiles(), 2], FP32))
        rank = ctx.enter_context(nc.sbuf_tensor("rank", [P, tiles(), 2], FP32))
        wts = ctx.enter_context(nc.sbuf_tensor("wts", [P, tiles(), 2], FP32))
        base = ctx.enter_context(nc.sbuf_tensor("base", [P, 2, NE], FP32))
        dest = ctx.enter_context(nc.sbuf_tensor("dest", [P, 2 * tiles()], I32))
        tabs = {n: ctx.enter_context(nc.sbuf_tensor("tab_" + n, [1, w], I32))
                for n, w in (("expert", blocks()), ("slot", blocks()), ("list", blocks()), ("end", NE))}
        mix_phase(nc, T, gb, const, cols, eid, rank, wts, base)
        with ExitStack() as of_experts:
            weights = (of_experts.enter_context(nc.sbuf_tensor("w13", [P, 2, W13], FP32)),
                       of_experts.enter_context(nc.sbuf_tensor("w2", [P, 2, W2], FP32)),
                       [of_experts.enter_context(nc.semaphore(f"expert_loaded{p}")) for p in range(2)])
            routing_phase(nc, T, cols, eid, rank, base, dest, tabs, weights)
            experts_phase(nc, T, const, tabs, weights)
        combine_phase(nc, T, dest, wts)




def matrices():
    import numpy as np
    i, j = np.arange(P)[:, None], np.arange(P)[None, :]
    same = i // SL == j // SL
    m = [i == j, i <= j, i > j, (i <= j) & same, (i > j) & same, i < j, i + j >= 0]
    m = [a.astype(np.float32) for a in m]
    for s in LEVELS:
        m.append(-((i // (2 * s) == j // (2 * s)) & (i // s < j // s)).astype(np.float32))
    return np.ascontiguousarray(np.stack(m, 1))


def kernel(**inputs):
    import numpy as np
    import concourse.bacc as bacc
    from concourse.bass_utils import run_bass_kernel_spmd

    a = {k: np.asarray(v) for k, v in inputs.items()}
    NT = tiles()

    def chunks(v):
        v = v.reshape(-1, P, *v.shape[1:])
        return np.swapaxes(v, 0, 1)

    def per_row(v):
        return np.broadcast_to(v.reshape(1, -1), (P, v.size))

    conv_w = np.concatenate([a["lru_conv_w"][0], a["gdn_conv_w"][0]], 1).T
    cols = {"ln1": chunks(a["ln1_g"][0]), "ln2": chunks(a["ln2_g"][0]), "cw": chunks(conv_w).reshape(P, -1),
            "cb": chunks(a["lru_conv_b"][0]), "ba": chunks(a["lru_ba"][0]), "bx": chunks(a["lru_bx"][0]),
            "lam": chunks(a["lru_lambda"][0]), "alog": per_row(a["gdn_a_log"][0]), "dtb": per_row(a["gdn_dt_bias"][0]),
            "ng": a["gdn_norm_g"][0][:, None],
            "rb": per_row(np.concatenate([a["router_group_b"][0], a["router_expert_b"][0]])),
            "iota": per_row(np.arange(NE, dtype=np.float32)),
            "stream": (np.arange(P)[:, None] // SL == np.arange(SB)).astype(np.float32)}
    conv_s = np.concatenate([a["state_lru_conv"][0], a["state_gdn_conv"][0]], 2)
    w13 = np.concatenate([a["moe_w1"][0], a["moe_w3"][0]], 2).reshape(NE, KD, P, 2 * FE).transpose(0, 2, 1, 3)
    w2 = a["moe_w2"][0].reshape(NE, FE // P, P, D).transpose(0, 2, 1, 3)
    arrays = {
        "x": np.concatenate([a["x_prompt"].reshape(-1, D), a["x_sample"].reshape(-1, D)]),
        "mats": matrices(),
        "cols": np.concatenate([cols[k] for k in COLS], 1),
        "conv_s": conv_s.transpose(2, 0, 1).reshape(CC, P, SB, 3).transpose(1, 0, 2, 3),
        "h_s": chunks(a["state_lru_h"][0].T),
        "S_s": a["state_gdn_S"][0].transpose(2, 0, 1, 3),
        "w_in": chunks(a["w_in"][0]),
        "gates": np.concatenate([a["lru_wa"], a["lru_wx"]]),
        "w_out": chunks(a["w_out"][0]),
        "router": np.pad(chunks(np.concatenate([a["router_group_w"][0], a["router_expert_w"][0]], 1)),
                         ((0, 0), (0, 0), (0, P - NGR - NE))),
        "ln2_row": a["ln2_g"].reshape(1, D), "final_row": a["final_g"].reshape(1, D),
        "w13": w13.reshape(NE, P, W13), "w2": w2.reshape(NE, P, W2),
        "tokens": np.arange(NT * P, dtype=np.int32).reshape(NT, P).T,
        "block_iota": np.arange(blocks(), dtype=np.float32).reshape(1, -1),
    }
    outs = {"out_y": (NT * P, D), "out_conv_p": (P, CC, 3), "out_h_p": (P, LC), "out_S_p": (P, HEADS, P),
            "out_conv_s": (P, CC, SB, 3), "out_h_s": (P, LC, SB), "out_S_s": (P, SB, HEADS, P)}
    scratch = {"mixin": ((P, FC, NT * P), FP32), "x2": ((NT * P, D), FP32), "h2": ((NT * P, D), FP32),
               "table": ((NE * NT * P + P, 1), I32), "y": ((blocks() * P, D), FP32)}
    nc = bacc.Bacc("TRN2", target_bir_lowering=False, num_devices=1)
    T, feeds = {}, {}
    for name, v in arrays.items():
        v = np.ascontiguousarray(v)
        feeds["in_" + name] = v
        T[name] = nc.dram_tensor("in_" + name, list(v.shape), mybir.dt.from_np(v.dtype), kind="ExternalInput").ap()
    for name, shape in outs.items():
        T[name] = nc.dram_tensor(name, list(shape), FP32, kind="ExternalOutput").ap()
    for name, (shape, dt) in scratch.items():
        T[name] = nc.dram_tensor(name, list(shape), dt).ap()
    build(nc, T)
    r = run_bass_kernel_spmd(nc, [feeds], core_ids=[0]).results[0]

    def conv(v, b):
        v = np.asarray(v).reshape(P, CC, b, 3).transpose(2, 3, 1, 0)
        return (np.ascontiguousarray(v[:, :, :LC].reshape(1, b, 3, LC * P)),
                np.ascontiguousarray(v[:, :, LC:].reshape(1, b, 3, QC * P)))

    def hidden(v, b):
        return np.ascontiguousarray(np.asarray(v).reshape(P, LC, b).transpose(2, 1, 0).reshape(1, b, LC * P))

    y = np.asarray(r["out_y"])
    lp, gp = conv(r["out_conv_p"], 1)
    ls, gs = conv(r["out_conv_s"], SB)
    Sp = np.ascontiguousarray(np.asarray(r["out_S_p"]).transpose(1, 0, 2)[None, None])
    Ss = np.ascontiguousarray(np.asarray(r["out_S_s"]).transpose(1, 2, 0, 3)[None])
    return (np.ascontiguousarray(y[:SEQ].reshape(1, SEQ, D)), np.ascontiguousarray(y[SEQ:].reshape(SB, SL, D)),
            lp, hidden(r["out_h_p"], 1), gp, Sp, ls, hidden(r["out_h_s"], SB), gs, Ss)
```
